# Optimizing a Trainium2 kernel written in Bass

```python
import math
import jax, jax.numpy as jnp
from jax import lax
import numpy as np

D_MODEL = 1024
BATCH = 1
SEQ = 256
DEPTH = 2

CHUNK = 64
N_MIXERS = 2
N_HEADS_A = 16
HEAD_DIM_A = D_MODEL // N_HEADS_A
LEFT_CHUNKS = 8
BAND = (LEFT_CHUNKS + 1) * CHUNK
REL_CLIP = 128
N_HEADS_B = 16
HEAD_DIM_B = D_MODEL // N_HEADS_B
SB_BLOCK = 128
D_FF = 2816
ALPHA = (2.0 * DEPTH) ** 0.25
BETA = (8.0 * DEPTH) ** -0.25
LN_EPS = 1e-5
N_A_LAYERS = (DEPTH + N_MIXERS - 1) // N_MIXERS
N_B_LAYERS = DEPTH // N_MIXERS

kernel_name = "hybrid_chunked_relbias_stickbreaking_macaron_deepnorm"

def layer_norm(x, g, b):
    xf = x.astype(jnp.float32)
    mu = jnp.mean(xf, axis=-1, keepdims=True)
    var = jnp.mean(jnp.square(xf - mu), axis=-1, keepdims=True)
    y = (xf - mu) * lax.rsqrt(var + LN_EPS)
    return (y * g.astype(jnp.float32) + b.astype(jnp.float32)).astype(x.dtype)

def swiglu(x, w_gate, w_up, w_down):
    return (jax.nn.silu(x @ w_gate) * (x @ w_up)) @ w_down

def rel_bias_band(rel_table):
    i = np.arange(CHUNK)[:, None]
    j = np.arange(BAND)[None, :]
    rel = (np.clip(i - j + LEFT_CHUNKS * CHUNK, -REL_CLIP, REL_CLIP) + REL_CLIP).astype(np.int32)
    return jnp.transpose(rel_table[rel], (2, 0, 1))

def chunked_rel_attention(x, w_qkv, w_o, rel_table):
    B, S, _ = x.shape
    n_chunks = S // CHUNK
    qkv = (x @ w_qkv).reshape(B, S, 3, N_HEADS_A, HEAD_DIM_A)
    q, k, v = qkv[:, :, 0], qkv[:, :, 1], qkv[:, :, 2]
    pad = LEFT_CHUNKS * CHUNK
    k_pad = jnp.pad(k, ((0, 0), (pad, 0), (0, 0), (0, 0)))
    v_pad = jnp.pad(v, ((0, 0), (pad, 0), (0, 0), (0, 0)))
    bias = rel_bias_band(rel_table).astype(jnp.float32)
    key_offset = jnp.arange(BAND) - pad
    scale = HEAD_DIM_A ** -0.5

    def one_chunk(c):
        start = c * CHUNK
        q_c = lax.dynamic_slice_in_dim(q, start, CHUNK, axis=1)
        k_c = lax.dynamic_slice_in_dim(k_pad, start, BAND, axis=1)
        v_c = lax.dynamic_slice_in_dim(v_pad, start, BAND, axis=1)
        s = jnp.einsum('bqhd,bkhd->bhqk', q_c, k_c,
                       preferred_element_type=jnp.float32) * scale + bias
        valid = (start + key_offset) >= 0
        s = jnp.where(valid[None, None, None, :], s, -jnp.inf)
        p = jax.nn.softmax(s, axis=-1).astype(v_c.dtype)
        return jnp.einsum('bhqk,bkhd->bqhd', p, v_c)

    out = lax.map(one_chunk, jnp.arange(n_chunks))
    out = jnp.transpose(out, (1, 0, 2, 3, 4)).reshape(B, S, D_MODEL)
    return out @ w_o

def stick_breaking_attention(x, w_qkv, w_o):
    B, S, _ = x.shape
    qkv = (x @ w_qkv).reshape(B, S, 3, N_HEADS_B, HEAD_DIM_B)
    q, k, v = qkv[:, :, 0], qkv[:, :, 1], qkv[:, :, 2]
    scale = HEAD_DIM_B ** -0.5
    outs = []
    for blk in range(S // SB_BLOCK):
        q0 = blk * SB_BLOCK
        kv_len = q0 + SB_BLOCK
        q_b = q[:, q0:kv_len]
        k_b = k[:, :kv_len]
        v_b = v[:, :kv_len]
        z = jnp.einsum('bqhd,bkhd->bhqk', q_b, k_b,
                       preferred_element_type=jnp.float32) * scale
        t_pos = q0 + jnp.arange(SB_BLOCK)[:, None]
        s_pos = jnp.arange(kv_len)[None, :]
        causal = s_pos < t_pos
        log_beta = jnp.where(causal, jax.nn.log_sigmoid(z), -jnp.inf)
        log_1m_beta = jnp.where(causal, jax.nn.log_sigmoid(-z), 0.0)
        stick = lax.cumsum(log_1m_beta, axis=log_1m_beta.ndim - 1, reverse=True) - log_1m_beta
        a = jnp.exp(log_beta + stick).astype(v_b.dtype)
        outs.append(jnp.einsum('bhqk,bkhd->bqhd', a, v_b))
    out = jnp.concatenate(outs, axis=1).reshape(B, S, D_MODEL)
    return out @ w_o

def setup_inputs(seed: int = 0) -> dict:
    key = jax.random.key(seed)
    ks = jax.random.split(key, 16)
    d_sc = D_MODEL ** -0.5
    f_sc = D_FF ** -0.5
    x = jax.random.normal(ks[0], (BATCH, SEQ, D_MODEL), jnp.float32)

    def qkv_weights(k, n):
        kq, kk, kv = jax.random.split(k, 3)
        wq = jax.random.normal(kq, (n, D_MODEL, D_MODEL), jnp.float32) * d_sc
        wk = jax.random.normal(kk, (n, D_MODEL, D_MODEL), jnp.float32) * d_sc
        wv = jax.random.normal(kv, (n, D_MODEL, D_MODEL), jnp.float32) * (d_sc * BETA)
        return jnp.concatenate([wq, wk, wv], axis=-1)

    w_qkv_a = qkv_weights(ks[1], N_A_LAYERS)
    w_o_a = jax.random.normal(ks[2], (N_A_LAYERS, D_MODEL, D_MODEL), jnp.float32) * (d_sc * BETA)
    rel_bias = jax.random.normal(ks[3], (2 * REL_CLIP + 1, N_HEADS_A), jnp.float32) * 0.5
    w_qkv_b = qkv_weights(ks[4], N_B_LAYERS)
    w_o_b = jax.random.normal(ks[5], (N_B_LAYERS, D_MODEL, D_MODEL), jnp.float32) * (d_sc * BETA)
    ffn_w_gate = jax.random.normal(ks[6], (DEPTH, 2, D_MODEL, D_FF), jnp.float32) * d_sc
    ffn_w_up = jax.random.normal(ks[7], (DEPTH, 2, D_MODEL, D_FF), jnp.float32) * d_sc
    ffn_w_down = jax.random.normal(ks[8], (DEPTH, 2, D_FF, D_MODEL), jnp.float32) * (f_sc * BETA)
    ln_g = 1.0 + 0.02 * jax.random.normal(ks[9], (DEPTH, 3, D_MODEL), jnp.float32)
    ln_b = 0.02 * jax.random.normal(ks[10], (DEPTH, 3, D_MODEL), jnp.float32)
    return {"x": x, "w_qkv_a": w_qkv_a, "w_o_a": w_o_a, "rel_bias": rel_bias,
            "w_qkv_b": w_qkv_b, "w_o_b": w_o_b, "ffn_w_gate": ffn_w_gate,
            "ffn_w_up": ffn_w_up, "ffn_w_down": ffn_w_down, "ln_g": ln_g, "ln_b": ln_b}

def reference(x, w_qkv_a, w_o_a, rel_bias, w_qkv_b, w_o_b, ffn_w_gate, ffn_w_up,
              ffn_w_down, ln_g, ln_b):
    for i in range(DEPTH):
        h = swiglu(x, ffn_w_gate[i, 0], ffn_w_up[i, 0], ffn_w_down[i, 0])
        x = layer_norm(ALPHA * x + 0.5 * h, ln_g[i, 0], ln_b[i, 0])
        j = i // N_MIXERS
        if i % N_MIXERS == 0:
            y = chunked_rel_attention(x, w_qkv_a[j], w_o_a[j], rel_bias)
        else:
            y = stick_breaking_attention(x, w_qkv_b[j], w_o_b[j])
        x = layer_norm(ALPHA * x + y, ln_g[i, 1], ln_b[i, 1])
        h = swiglu(x, ffn_w_gate[i, 1], ffn_w_up[i, 1], ffn_w_down[i, 1])
        x = layer_norm(ALPHA * x + 0.5 * h, ln_g[i, 2], ln_b[i, 2])
    return x


_drawn_inputs = setup_inputs


def setup_inputs(seed=0):
    import zlib

    import numpy as np

    out = dict(_drawn_inputs(seed))
    spreads = {}
    factors = {'rel_bias': 4.443}
    for name, (base, spread) in spreads.items():
        noise = np.random.default_rng([zlib.crc32(name.encode()), seed]).standard_normal(out[name].shape)
        drawn = base * np.exp(spread * noise) if base else spread * noise
        out[name] = __import__('jax').numpy.asarray(drawn.astype(out[name].dtype))
    for name, factor in factors.items():
        out[name] = (out[name] * factor).astype(out[name].dtype)
    return out
```

```python
from contextlib import ExitStack

import concourse.bass as bass
from concourse import mybir

F32 = mybir.dt.float32
F32R = mybir.dt.float32r
ALU = mybir.AluOpType
ACT = mybir.ActivationFunctionType
AX_X = mybir.AxisListType.X

P = 128
SEQ, D, FF, HEADS, HD = 256, 1024, 2816, 16, 64
DEPTH = 2
ROWS = SEQ // P
KD = D // P
KF = FF // P
HALF = D // 2
CHUNK_F = 256
CHUNKS = FF // CHUNK_F
CLIP = 128
ATT_CHUNK = 64
GROUP = 4
GROUPS = HEADS // GROUP
PAIRS = HEADS // 2
SCALE = HD ** -0.5
ALPHA = (2.0 * DEPTH) ** 0.25
EPS = 1e-5
MASKED = -1e30
HELD = 3

RAW = 4
SPLIT = 5
UNITS_FFN = 2 * CHUNKS + KF // 2
UNITS_MIX = 4 * GROUPS
FFN_UNIT = [0, UNITS_FFN + UNITS_MIX, 2 * UNITS_FFN + UNITS_MIX, 3 * UNITS_FFN + 2 * UNITS_MIX]
MIX_UNIT = [UNITS_FFN, 3 * UNITS_FFN + UNITS_MIX]
UNITS = 4 * UNITS_FFN + 2 * UNITS_MIX
FFN_NORM = [0, 2, 3, 5]
MIX_NORM = [1, 4]
NORMS = 3 * DEPTH
NORM_UNIT = [MIX_UNIT[0], FFN_UNIT[1], FFN_UNIT[2], MIX_UNIT[1], FFN_UNIT[3], UNITS]
NORM_SCALE = [(2 * ALPHA, 4 * EPS), (ALPHA, EPS), (2 * ALPHA, 4 * EPS)] * DEPTH

FFN_SLOTS = [j % 4 for j in range(24)] + [4, 0, 1, 2, 3, 0, 4, 2, 3]
MIX_SLOTS = [j % SPLIT for j in range(15)] + [2]
SLOT = (FFN_SLOTS + MIX_SLOTS + FFN_SLOTS) * DEPTH
assert len(SLOT) == UNITS and len(FFN_SLOTS) == UNITS_FFN and len(MIX_SLOTS) == UNITS_MIX


def former(n):
    return max((k for k in range(n) if SLOT[k] == SLOT[n]), default=None)


MIX_ORDER = ([("v", 0), ("v", 1), ("q", 0), ("k", 0), ("q", 1), ("k", 1)]
             + [(what, g) for g in range(2, GROUPS) for what in "vqk"] + [("o", g) for g in range(GROUPS)])
BLOCKS = ([("v", 0, 0), ("v", 1, 0), ("v", 0, 1), ("v", 1, 1)]
          + [(what, g, b) for what, g in MIX_ORDER[2:3 * GROUPS] for b in range(2)])
FIRST_BLOCKS = 8

KEYS = 384
SPANS = [(256, 384), (0, 256)]
DIAG = 128


def build(nc, x_in, w_qkv, w_o, rel_bias, w_gate, w_up, w_down, ln_g, ln_b, table, out):
    with ExitStack() as ctx:
        def sb(name, shape, dt=F32):
            return ctx.enter_context(nc.sbuf_tensor(name, shape, dt))

        def sem(name):
            return ctx.enter_context(nc.semaphore(name))

        raw = [sb(f"raw{s}", [P, 2048]) for s in range(RAW)]
        w_hi = [sb(f"w_hi{s}", [P, 2048], F32R) for s in range(SPLIT)]
        w_lo = [sb(f"w_lo{s}", [P, 2048], F32R) for s in range(SPLIT)]
        x = sb("x", [P, ROWS, D])
        xT_hi = sb("xT_hi", [P, KD, SEQ], F32R)
        xT_lo = sb("xT_lo", [P, KD, SEQ], F32R)
        hT_at = nc.sbuf_base
        hT_hi = sb("hT_hi", [P, KF, SEQ], F32R)
        hT_lo = sb("hT_lo", [P, KF, SEQ], F32R)
        assert nc.sbuf_base - hT_at == 2 * KF * SEQ * 4
        place = [hT_at + PAIRS * SEQ * 4, hT_at + (KF + PAIRS) * SEQ * 4]
        room = [hT_at + KF * SEQ * 4, hT_at + 2 * KF * SEQ * 4]

        def in_hT(which, name, shape):
            size = 4 * shape[1] * shape[2]
            place[which] += size
            assert place[which] <= room[which]
            return nc.alloc_sbuf_tensor_at(name, shape, F32, offset=place[which] - size)

        qT = [in_hT(0, f"qT{g}", [P, 2, SEQ]) for g in range(2)]
        kT = [in_hT(0, f"kT{g}", [P, 2, SEQ]) for g in range(2)]
        v = [in_hT(0, f"v{g}", [P, ROWS, GROUP * HD]) for g in range(2)]
        probs = [in_hT(1, f"probs{p}", [P, 2, KEYS]) for p in range(2)]
        stick = in_hT(1, "stick", [P, 2, KEYS])
        probsT = in_hT(1, "probsT", [P, 2, KEYS])
        gate_act = sb("gate_act", [P, ROWS, CHUNK_F])
        hidden = sb("hidden", [P, ROWS, CHUNK_F])
        gain = sb("gain", [P, D])
        shift = sb("shift", [P, D])
        rel = [sb(f"rel{p}", [P, 2, 2 * P]) for p in range(2)]
        ident = sb("ident", [P, P])
        restart = sb("restart", [P, KEYS])
        stats = sb("stats", [P, 2, 6])
        mean_var = sb("mean_var", [P, 2])
        var_eps = sb("var_eps", [P, 1])
        rstd = sb("rstd", [P, 1])
        power = sb("power", [P, 1])
        top = sb("top", [P, 2, 4])
        neg_top = sb("neg_top", [P, 2, 4])
        total = sb("total", [P, 2, 4])
        inv_total = sb("inv_total", [P, 2, 4])
        ones = sb("ones", [1, P])
        tab = sb("tab", [P, 3, HEADS])
        tab_row = sb("tab_row", [HEADS, 3 * P])

        psum = ctx.enter_context(nc.psum_tensor("psum", [P, 8, 512], F32))
        GU = [[psum[:, 0, :], psum[:, 1, :]], [psum[:, 2, :], psum[:, 3, :]]]
        TURN = psum[:, 4, :]
        Y = [[psum[:, 5, :], psum[:, 6, :]], [psum[:, 7, :], psum[:, 3, :]]]
        XT = [psum[:, 4, :], psum[:, 1, :]]
        SCORES = psum[:, 0:2, 0:KEYS]
        HEADOUT = psum[:, 4, 0:SEQ]

        def PROJ(i):
            return psum[:, 0 if i == 1 else 2 + i % 2, 0:SEQ]

        raw_loaded = [sem(f"raw_loaded{s}") for s in range(RAW)]
        hi_done, lo_done, unit_used = sem("hi_done"), sem("lo_done"), sem("unit_used")
        first_loaded, first_hi, first_lo = sem("first_loaded"), sem("first_hi"), sem("first_lo")
        x_loaded = [sem(f"x_loaded{r}") for r in range(ROWS)]
        norm_loaded = sem("norm_loaded")
        xT_psum, xT_hi_done, xT_lo_done = sem("xT_psum"), sem("xT_hi_done"), sem("xT_lo_done")
        gu_done = sem("gu_done")
        silu_done, hidden_done = sem("silu_done"), sem("hidden_done")
        hT_psum, hT_hi_done, hT_lo_done = sem("hT_psum"), sem("hT_hi_done"), sem("hT_lo_done")
        y_done = sem("y_done")
        resid_done = sem("resid_done")
        stats_done, mean_done, eps_done = sem("stats_done"), sem("mean_done"), sem("eps_done")
        rstd_done = sem("rstd_done")
        gained_done, x_ready = sem("gained_done"), sem("x_ready")
        proj_done = sem("proj_done")
        proj_copied = sem("proj_copied")
        scores_done = sem("scores_done")
        biased_done, neg_top_done, exp_done, inv_done = (sem("biased_done"), sem("neg_top_done"),
                                                         sem("exp_done"), sem("inv_done"))
        sigmoid_done, masked_done, stick_done = sem("sigmoid_done"), sem("masked_done"), sem("stick_done")
        probs_ready, probsT_psum, probsT_done = sem("probs_ready"), sem("probsT_psum"), sem("probsT_done")
        headout_done, headout_hi, headout_lo = sem("headout_done"), sem("headout_hi"), sem("headout_lo")
        rel_loaded = [sem(f"rel_loaded{p}") for p in range(2)]
        tab_loaded, tab_psum, tab_copied, tab_stored = (sem("tab_loaded"), sem("tab_psum"),
                                                        sem("tab_copied"), sem("tab_stored"))
        const_set, const_ready = sem("const_set"), sem("const_ready")
        stored = sem("stored")

        block = ctx.enter_context(nc.Block())

        def as_gu(t):
            return t[:].rearrange("p (k n) -> p k n", k=KD // 2)

        def as_qkv(t):
            return t[:].rearrange("p (k n) -> p k n", k=KD)

        def as_rows(t):
            return t[:].rearrange("p (k n) -> p k n", k=2)

        def wait_block(eng, m, i):
            what, g, b = BLOCKS[i]
            if b == 0:
                eng.wait_ge(proj_done, m * 3 * GROUPS + sum(x[2] == 0 for x in BLOCKS[:i + 1]))
            else:
                eng.wait_ge(unit_used, MIX_UNIT[m] + MIX_ORDER.index((what, g)) + 1)

        def fillers(g):
            if g == GROUPS - 1:
                todo = [("o", n // 4, n // 2 % 2, n % 2) for n in range(10)]
                return (todo[0:5], 4), (todo[5:10], 4)
            if g == 0:
                todo = BLOCKS[FIRST_BLOCKS:FIRST_BLOCKS + 4]
                return (todo[0:2], None), (todo[2:4], None)
            at = FIRST_BLOCKS + 4 + 6 * (g - 1)
            todo = BLOCKS[at:at + 6]
            return (todo[0:3], 2), (todo[3:6], 2)

        @block.sync
        def _(sp):
            def slot_free(n):
                sp.wait_ge(lo_done, n - RAW + 1)

            def load_gate_up(f, c, n, slot, wait, khs=(0, 1)):
                for kh in khs:
                    s = (slot + kh) % RAW
                    if wait:
                        slot_free(n + kh)
                    dst = as_gu(raw[s])
                    for w, at in ((w_gate, 0), (w_up, CHUNK_F)):
                        src = w[f // 2, f % 2, kh * HALF:(kh + 1) * HALF, bass.ds(c * CHUNK_F, CHUNK_F)]
                        sp.dma_start(dst[:, :, at:at + CHUNK_F],
                                     src.rearrange("(k p) n -> p k n", p=P)).then_inc(raw_loaded[s], 16)

            def load_first():
                for part in range(2):
                    k = slice(2 * part, 2 * part + 2)
                    for w, at in ((w_gate, 0), (w_up, CHUNK_F)):
                        src = w[0, 0, 2 * part * P:(2 * part + 2) * P, 0:CHUNK_F]
                        sp.dma_start(as_gu(raw[0])[:, k, at:at + CHUNK_F], src.rearrange("(k p) n -> p k n", p=P)
                                     ).then_inc((first_loaded, raw_loaded[0])[part], 16)
                sp.dma_start(x[:, 1, :], x_in[0, P:SEQ, :]).then_inc(x_loaded[1], 16)

            def load_rows(w, k0, n):
                s = n % RAW
                slot_free(n)
                for kk in range(2):
                    sp.dma_start(as_rows(raw[s])[:, kk, :],
                                 w[(k0 + kk) * P:(k0 + kk + 1) * P, :]).then_inc(raw_loaded[s], 16)

            def load_ffn(f):
                n0 = FFN_UNIT[f]
                for c in range(2):
                    first = n0 + 2 * c == 0
                    if first:
                        load_first()
                    load_gate_up(f, c, n0 + 2 * c, n0 + 2 * c, n0 + 2 * c >= RAW, (1,) if first else (0, 1))
                with sp.Fori(1, CHUNKS // 2) as i:
                    for cc in range(2):
                        load_gate_up(f, i * 2 + cc, i * 4 + (n0 + 2 * cc), n0 + 2 * cc, wait=True)
                c = CHUNKS - 1
                load_gate_up(f, c, n0 + 2 * c, n0 + 2 * c, wait=True)
                for d in range(KF // 2):
                    load_rows(w_down[f // 2, f % 2], 2 * d, n0 + 2 * CHUNKS + d)

            def load_mixer(m):
                for u in range(UNITS_MIX):
                    n = MIX_UNIT[m] + u
                    what, g = MIX_ORDER[u]
                    if what == "o":
                        load_rows(w_o[m], 2 * g, n)
                        continue
                    s = n % RAW
                    slot_free(n)
                    at = "qkv".index(what) * D + g * GROUP * HD
                    for kh in range(2):
                        src = w_qkv[m][kh * HALF:(kh + 1) * HALF, at:at + GROUP * HD]
                        sp.dma_start(as_qkv(raw[s])[:, kh * 4:kh * 4 + 4, :],
                                     src.rearrange("(k p) n -> p k n", p=P)).then_inc(raw_loaded[s], 16)

            for m in range(DEPTH):
                load_ffn(2 * m)
                load_mixer(m)
                load_ffn(2 * m + 1)
            for r in range(ROWS):
                for half in range(2):
                    sp.wait_ge(x_ready, ((NORMS - 1) * ROWS + r) * 2 + half + 1)
                    rows, cols = slice(r * P, (r + 1) * P), slice(half * HALF, (half + 1) * HALF)
                    sp.dma_start(out[0, rows, cols], x[:, r, cols]).then_inc(stored, 16)
            sp.wait_ge(stored, 2 * 16 * ROWS)

        @block.tensor
        def _(pe):
            def unit_ready(n):
                pe.wait_ge(lo_done, n + 1)

            def transpose_x(t, r):
                for hb in range(2):
                    if t == 0:
                        pe.wait_ge(x_loaded[r], 16)
                    else:
                        pe.wait_ge(x_ready, ((t - 1) * ROWS + r) * 2 + hb + 1)
                    if r > 0:
                        pe.wait_ge(xT_lo_done, 4 * t + hb + 1)
                    for k in range(4):
                        kk = 4 * hb + k
                        last = pe.transpose(XT[hb][:, k * P:(k + 1) * P], x[:, r, kk * P:(kk + 1) * P], ident[:])
                    last.then_inc(xT_psum, 1)

            def xT_ready(t, r):
                pe.wait_ge(xT_lo_done, 4 * t + 2 * r + 2)

            def three(acc, st, mv, first, last):
                pe.matmul(acc, st[0], mv[0], start=first, stop=False)
                pe.matmul(acc, st[1], mv[0], start=False, stop=False)
                return pe.matmul(acc, st[0], mv[1], start=False, stop=last)

            def static_zero(n):
                return isinstance(n, int) and n == 0

            def gate_up(r, par, slot, n, release, between=None):
                for kh in range(2):
                    s = (slot + kh) % 4
                    if not release and not (static_zero(n) and kh == 0):
                        unit_ready(n + kh)
                    for k in range(4):
                        kk = 4 * kh + k
                        if static_zero(n) and not release and kk in (0, 2):
                            pe.wait_ge((first_lo, lo_done)[kk // 2], 1)
                        if between and kk == KD - 2:
                            between()
                        rows = slice(r * P, (r + 1) * P)
                        last = three(GU[par][r], (xT_hi[:, kk, rows], xT_lo[:, kk, rows]),
                                     (as_gu(w_hi[s])[:, k, :], as_gu(w_lo[s])[:, k, :]), kk == 0, kk == KD - 1)
                    if release and kh == 0:
                        last.then_inc(unit_used, 1)
                return last

            def turn_hidden(h_wait):
                pe.wait_ge(hidden_done, h_wait)
                for j in range(2):
                    for r in range(ROWS):
                        last = pe.transpose(TURN[:, (2 * j + r) * P:(2 * j + r + 1) * P],
                                            hidden[:, r, j * P:(j + 1) * P], ident[:])
                last.then_inc(hT_psum, 1)

            def chunk_in_loop(f, i, cc):
                n0 = FFN_UNIT[f]
                n, par, slot = i * 4 + (n0 + 2 * cc), cc % 2, 2 * cc
                gate_up(0, par, slot, n, False).then_inc(gu_done, 1)
                turn_hidden(i * 4 + (f * CHUNKS * ROWS + 2 * cc))
                gate_up(1, par, slot, n, True).then_inc(unit_used, 1)

            def half_block(r, half, d, n, count):
                s = SLOT[n]
                rows, cols = slice(r * P, (r + 1) * P), slice(half * HALF, (half + 1) * HALF)
                for kk in range(2):
                    k = 2 * d + kk
                    last = three(Y[r][half], (hT_hi[:, k, rows], hT_lo[:, k, rows]),
                                 (as_rows(w_hi[s])[:, kk, cols], as_rows(w_lo[s])[:, kk, cols]),
                                 k == 0, k == 2 * count - 1)
                return last

            def ffn_matmul(f, t, finish):
                n0 = FFN_UNIT[f]
                xT_ready(t, 0)
                gate_up(0, 0, 0, n0, False, lambda: transpose_x(t, 1)).then_inc(gu_done, 1)
                if f == 0:
                    relative_table()
                xT_ready(t, 1)
                gate_up(1, 0, 0, n0, True).then_inc(unit_used, 1)
                with pe.Fori(0, CHUNKS // 2) as i:
                    for cc in (1, 2):
                        chunk_in_loop(f, i, cc)
                n0, count = n0 + 2 * CHUNKS, KF // 2
                for d in range(count - HELD):
                    unit_ready(n0 + d)
                    if d == 0:
                        pe.wait_ge(hidden_done, (f * CHUNKS + CHUNKS - 1) * ROWS)
                    if d == 1:
                        turn_hidden((f + 1) * CHUNKS * ROWS)
                    pe.wait_ge(hT_lo_done, f * CHUNKS + d + 1)
                    for r in range(ROWS):
                        for half in range(2):
                            last = half_block(r, half, d, n0 + d, count)
                    last.then_inc(unit_used, 1)
                pe.wait_ge(hT_lo_done, (f + 1) * CHUNKS)
                for r in range(ROWS):
                    for half in range(2):
                        for d in range(count - HELD, count):
                            if r == 0 and half == 0:
                                unit_ready(n0 + d)
                            if r == 1 and half == 1 and d == count - 2:
                                finish()
                            last = half_block(r, half, d, n0 + d, count)
                            if r == 1 and half == 1:
                                last.then_inc(unit_used, 1)
                        if not (r == 1 and half == 1):
                            last.then_inc(y_done, 1)

            def proj_block(m, i, between=None):
                what, g, b = BLOCKS[i]
                n = MIX_UNIT[m] + MIX_ORDER.index((what, g))
                hi, lo = as_qkv(w_hi[SLOT[n]]), as_qkv(w_lo[SLOT[n]])
                if b == 0:
                    unit_ready(n)
                if i >= 2:
                    pe.wait_ge(proj_copied, m * len(BLOCKS) + i - 1)
                acc = PROJ(i)
                part = slice(b * P, (b + 1) * P)
                for k in range(KD):
                    if between and k == KD - 3:
                        between()
                    if what == "v":
                        last = three(acc, (xT_hi[:, k, part], xT_lo[:, k, part]), (hi[:, k, :], lo[:, k, :]),
                                     k == 0, k == KD - 1)
                    else:
                        last = three(acc, (hi[:, k, part], lo[:, k, part]), (xT_hi[:, k, :], xT_lo[:, k, :]),
                                     k == 0, k == KD - 1)
                last.then_inc(proj_done if b == 0 else unit_used, 1)

            def out_half(m, g, r, half):
                n = MIX_UNIT[m] + 3 * GROUPS + g
                if half == 0:
                    unit_ready(n)
                    pe.wait_ge(headout_lo, m * PAIRS + 2 * g + 2)
                last = half_block(r, half, g, n, GROUPS)
                if (r, half) == (1, 1):
                    last.then_inc(unit_used, 1)
                elif g == GROUPS - 1:
                    last.then_inc(y_done, 1)

            def scores(m, pp):
                g, p = pp // 2, pp % 2
                pe.wait_ge(proj_copied, m * len(BLOCKS) + BLOCKS.index(("k", g, 1)) + 1)
                if m * PAIRS + pp > 0:
                    pe.wait_ge(probsT_done, m * PAIRS + pp)
                q, k = qT[g % 2], kT[g % 2]
                for h in range(2):
                    part = slice(h * HD, (h + 1) * HD)
                    for r, (a, b) in enumerate(SPANS):
                        last = pe.matmul(SCORES[:, h, a:b], q[part, p, r * P:(r + 1) * P], k[part, p, 0:b - a],
                                         start=True, stop=True)
                last.then_inc(scores_done, 1)

            def turn_probs(m, pp):
                pe.wait_ge(probs_ready, m * PAIRS + pp + 1)
                pr = probs[pp % 2]
                for h in range(2):
                    for to, at in ((0, 2 * P), (P, 0), (2 * P, P)):
                        last = pe.transpose(SCORES[:, h, to:to + P], pr[:, h, at:at + P], ident[:])
                last.then_inc(probsT_psum, 1)

            def head_out(m, pp):
                g, p = pp // 2, pp % 2
                pe.wait_ge(probsT_done, m * PAIRS + pp + 1)
                if m * PAIRS + pp > 0:
                    pe.wait_ge(headout_lo, m * PAIRS + pp)
                for h in range(2):
                    acc = HEADOUT[h * HD:(h + 1) * HD, :]
                    cols = slice((2 * p + h) * HD, (2 * p + h + 1) * HD)
                    pe.matmul(acc, v[g % 2][:, 0, cols], probsT[:, h, 0:2 * P], start=True, stop=False)
                    last = pe.matmul(acc[:, P:2 * P], v[g % 2][:, 1, cols], probsT[:, h, 2 * P:3 * P],
                                     start=False, stop=True)
                last.then_inc(headout_done, 1)

            def mixer_matmul(m, t, finish):
                xT_ready(t, 0)
                proj_block(m, 0)
                proj_block(m, 1)
                transpose_x(t, 1)
                xT_ready(t, 1)
                for i in range(2, FIRST_BLOCKS):
                    proj_block(m, i)
                for g in range(GROUPS):
                    for p in range(2):
                        scores(m, 2 * g + p)
                        todo, turn = fillers(g)[p]
                        for j, block in enumerate(todo):
                            if j == turn:
                                turn_probs(m, 2 * g + p)
                            if block[0] == "o":
                                out_half(m, *block[1:])
                            elif turn is None and j == 1:
                                proj_block(m, BLOCKS.index(block), lambda: turn_probs(m, 2 * g + p))
                            else:
                                proj_block(m, BLOCKS.index(block))
                        head_out(m, 2 * g + p)
                last_g = GROUPS - 1
                for half in range(2):
                    out_half(m, last_g, 0, half)
                for half in range(2):
                    out_half(m, last_g - 1, 1, half)
                out_half(m, last_g, 1, 0)
                finish()
                out_half(m, last_g, 1, 1)

            def relative_table():
                pe.wait_ge(tab_loaded, 48)
                pe.matmul(Y[0][0][0:HEADS, 0:P], tab[:, 0, :], ident[:], start=True, stop=True)
                pe.matmul(Y[0][0][0:HEADS, P:2 * P], tab[:, 1, :], ident[:], start=True, stop=True)
                pe.matmul(Y[0][0][0:HEADS, 2 * P:3 * P], tab[0:1, 2, :], ones[:], start=True,
                          stop=True).then_inc(tab_psum, 1)

            pe.wait_ge(const_ready, 2)
            transpose_x(0, 0)
            for m in range(DEPTH):
                t = 3 * m
                ffn_matmul(2 * m, t, lambda: transpose_x(t + 1, 0))
                mixer_matmul(m, t + 1, lambda: transpose_x(t + 2, 0))
                ffn_matmul(2 * m + 1, t + 2, lambda: transpose_x(t + 3, 0) if m < DEPTH - 1 else None)

        @block.scalar
        def _(act):
            def hi_part(n, raw_slot, count, slot, before):
                act.wait_ge(raw_loaded[raw_slot], count * 32)
                if before is not None:
                    act.wait_ge(unit_used, before + 1)
                act.activation(w_hi[slot][:], raw[raw_slot][:], ACT.Copy).then_inc(hi_done, 1)

            def hi_unit(n):
                if n < UNITS:
                    hi_part(n, n % RAW, n // RAW + 1, SLOT[n], former(n))

            def hi_first():
                for part in range(2):
                    act.wait_ge((first_loaded, raw_loaded[0])[part], 32)
                    cols = slice(1024 * part, 1024 * part + 1024)
                    act.activation(w_hi[0][:, cols], raw[0][:, cols], ACT.Copy).then_inc((first_hi, hi_done)[part], 1)

            def silu(f, c, r, par, again=True):
                idx = c * 2 + (f * CHUNKS * ROWS + r)
                if r == 0:
                    act.wait_ge(gu_done, c + (f * CHUNKS + 1))
                else:
                    act.wait_ge(unit_used, c * 2 + (FFN_UNIT[f] + 2))
                if r == 0 and again:
                    act.wait_ge(hidden_done, idx - 1)
                act.activation(gate_act[:, r, :], GU[par][r][:, 0:CHUNK_F], ACT.Silu).then_inc(silu_done, 1)

            def hT_hi_part(f, c):
                act.wait_ge(hT_psum, c + (f * CHUNKS + 1))
                act.activation(hT_hi[:, bass.ds(c * 2, 2), :], TURN.rearrange("p (k n) -> p k n", k=2),
                               ACT.Copy).then_inc(hT_hi_done, 1)

            def xT_hi_part(t, r):
                for hb in range(2):
                    act.wait_ge(xT_psum, 4 * t + 2 * r + hb + 1)
                    act.activation(xT_hi[:, 4 * hb:4 * hb + 4, r * P:(r + 1) * P],
                                   XT[hb].rearrange("p (k n) -> p k n", k=4), ACT.Copy).then_inc(xT_hi_done, 1)

            def ffn_scalar(f, t):
                n0 = FFN_UNIT[f]
                xT_hi_part(t, 1)
                hi_unit(n0 + 2)
                silu(f, 0, 0, 0, again=False)
                if f == 0:
                    relative_table()
                hi_unit(n0 + 3)
                with act.Fori(0, CHUNKS // 2) as i:
                    for cc in (1, 2):
                        c = i * 2 + cc
                        silu(f, c - 1, 1, (cc - 1) % 2)
                        for kh in range(2):
                            j = 2 * cc + 2 + kh
                            n = n0 + j
                            hi_part(i * 4 + n, n % RAW, i + (n // RAW + 1), j % 4, i * 4 + (n - 4))
                        silu(f, c, 0, cc % 2)
                        hT_hi_part(f, c - 1)
                silu(f, CHUNKS - 1, 1, 0)
                n0 += 2 * CHUNKS
                hi_unit(n0 + 2)
                hT_hi_part(f, CHUNKS - 1)
                for d in range(3, KF // 2 + 2):
                    hi_unit(n0 + d)

            def copy_proj(m, i):
                what, g, b = BLOCKS[i]
                wait_block(act, m, i)
                if g >= 2:
                    act.wait_ge(headout_done, m * PAIRS + 2 * (g - 1))
                dst = {"v": v, "q": qT, "k": kT}[what][g % 2]
                act.activation(dst[:, b, :], PROJ(i), ACT.Copy,
                               scale=SCALE if what == "q" else 1.0).then_inc(proj_copied, 1)

            def exps(m, pp):
                par = pp % 2
                act.wait_ge(neg_top_done, m * PAIRS + pp + 1)
                for h in range(2):
                    for r, (a, b) in enumerate(SPANS):
                        j = 2 * h + r
                        act.activation(probs[par][:, h, a:b], probs[par][:, h, a:b], ACT.Exp,
                                       bias=neg_top[:, par, j:j + 1],
                                       accum_out=total[:, par, j:j + 1]).then_inc(exp_done, 1)

            def sigmoids(m, pp):
                act.wait_ge(scores_done, m * PAIRS + pp + 1)
                if pp >= 2:
                    act.wait_ge(probsT_psum, m * PAIRS + pp - 1)
                act.activation(probs[pp % 2][:], SCORES, ACT.Sigmoid).then_inc(sigmoid_done, 1)
                if pp >= 1:
                    act.wait_ge(probs_ready, m * PAIRS + pp)
                act.activation(stick[:], SCORES, ACT.Sigmoid, scale=-1.0).then_inc(sigmoid_done, 1)

            def probsT_copy(m, pp):
                act.wait_ge(probsT_psum, m * PAIRS + pp + 1)
                if m * PAIRS + pp > 0:
                    act.wait_ge(headout_done, m * PAIRS + pp)
                act.activation(probsT[:], SCORES, ACT.Copy).then_inc(probsT_done, 1)

            def headout_hi_part(m, pp):
                act.wait_ge(headout_done, m * PAIRS + pp + 1)
                act.activation(hT_hi[:, pp, :], HEADOUT, ACT.Copy).then_inc(headout_hi, 1)

            def mixer_scalar(m, t):
                n0 = MIX_UNIT[m]
                weights = exps if m % 2 == 0 else sigmoids
                hi_unit(n0 + 2)
                copy_proj(m, 0)
                copy_proj(m, 1)
                xT_hi_part(t, 1)
                hi_unit(n0 + 3)
                copy_proj(m, 2)
                copy_proj(m, 3)
                hi_unit(n0 + 4)
                copy_proj(m, 4)
                copy_proj(m, 5)
                hi_unit(n0 + 5)
                copy_proj(m, 6)
                copy_proj(m, 7)
                ahead = iter(range(n0 + 6, n0 + UNITS_MIX + 1))

                def filler(todo):
                    if todo[0] != "o":
                        copy_proj(m, BLOCKS.index(todo))

                for g in range(GROUPS):
                    for p in range(2):
                        todo, pp = fillers(g)[p][0], 2 * g + p
                        softmax = m % 2 == 0
                        if p == 0 and softmax:
                            hi_unit(next(ahead))
                        weights(m, pp)
                        if p == 0 and not softmax:
                            hi_unit(next(ahead))
                        filler(todo[0])
                        early = softmax and p == 1 and 0 < g < GROUPS - 1
                        if early:
                            hi_unit(next(ahead))
                        if len(todo) > 2:
                            filler(todo[1])
                        probsT_copy(m, pp)
                        if not early and (p == 0 or g > 0):
                            hi_unit(next(ahead))
                        filler(todo[-1])
                        headout_hi_part(m, pp)
                hi_unit(n0 + UNITS_MIX + 1)

            def relative_table():
                act.wait_ge(tab_psum, 1)
                act.activation(tab_row[:], Y[0][0][0:HEADS, 0:3 * P], ACT.Copy).then_inc(tab_copied, 1)

            act.dma_start(x[:, 0, :], x_in[0, 0:P, :]).then_inc(x_loaded[0], 16)
            xT_hi_part(0, 0)
            hi_first()
            hi_unit(1)
            for m in range(DEPTH):
                ffn_scalar(2 * m, 3 * m)
                xT_hi_part(3 * m + 1, 0)
                mixer_scalar(m, 3 * m + 1)
                xT_hi_part(3 * m + 2, 0)
                ffn_scalar(2 * m + 1, 3 * m + 2)
                if m < DEPTH - 1:
                    xT_hi_part(3 * m + 3, 0)

        @block.vector
        def _(dve):
            def lo_part(n, raw_slot, slot):
                dve.wait_ge(hi_done, n + 1)
                dve.tensor_tensor(w_lo[slot][:], raw[raw_slot][:], w_hi[slot][:], ALU.subtract).then_inc(lo_done, 1)

            def lo_unit(n):
                if n < UNITS:
                    lo_part(n, n % RAW, SLOT[n])

            def lo_first():
                for part in range(2):
                    dve.wait_ge((first_hi, hi_done)[part], 1)
                    cols = slice(1024 * part, 1024 * part + 1024)
                    last = dve.tensor_tensor(w_lo[0][:, cols], raw[0][:, cols], w_hi[0][:, cols], ALU.subtract)
                    last.then_inc((first_lo, lo_done)[part], 1)

            def hidden_rows(f, c, r, par, first=False):
                idx = c * 2 + (f * CHUNKS * ROWS + r)
                dve.wait_ge(silu_done, idx + 1)
                if not first:
                    dve.wait_ge(hT_psum, c + f * CHUNKS)
                dve.tensor_tensor(hidden[:, r, :], GU[par][r][:, CHUNK_F:], gate_act[:, r, :],
                                  ALU.mult).then_inc(hidden_done, 1)

            def hT_lo_part(f, c):
                dve.wait_ge(hT_hi_done, c + (f * CHUNKS + 1))
                dve.tensor_tensor(hT_lo[:, bass.ds(c * 2, 2), :], TURN.rearrange("p (k n) -> p k n", k=2),
                                  hT_hi[:, bass.ds(c * 2, 2), :], ALU.subtract).then_inc(hT_lo_done, 1)

            def xT_lo_part(t, r):
                for hb in range(2):
                    dve.wait_ge(xT_hi_done, 4 * t + 2 * r + hb + 1)
                    dst = (slice(None), slice(4 * hb, 4 * hb + 4), slice(r * P, (r + 1) * P))
                    dve.tensor_tensor(xT_lo[dst], XT[hb].rearrange("p (k n) -> p k n", k=4), xT_hi[dst],
                                      ALU.subtract).then_inc(xT_lo_done, 1)

            def norm(l, r):
                scale, eps = NORM_SCALE[l]
                at = ROWS * l + r
                halves = [slice(half * HALF, (half + 1) * HALF) for half in range(2)]
                for half, cols in enumerate(halves):
                    if r == 1 and half == 1:
                        dve.wait_ge(unit_used, NORM_UNIT[l])
                    else:
                        dve.wait_ge(y_done, 3 * l + 2 * r + half + 1)
                    dve.scalar_tensor_tensor(x[:, r, cols], x[:, r, cols], scale, Y[r][half],
                                             ALU.mult, ALU.add).then_inc(resid_done, 1)
                    dve.wait_ge(resid_done, 2 * at + half + 1)
                    dve.bn_stats(stats[:, half, :], x[:, r, cols]).then_inc(stats_done, 1)
                dve.wait_ge(stats_done, 2 * at + 2)
                dve.bn_aggr(mean_var[:], stats[:].rearrange("p a b -> p (a b)")).then_inc(mean_done, 1)
                dve.wait_ge(mean_done, at + 1)
                dve.tensor_scalar(var_eps[:], mean_var[:, 1:2], eps, None, ALU.add).then_inc(eps_done, 1)
                dve.wait_ge(norm_loaded, 32 * (l + 1))
                for cols in halves:
                    dve.scalar_tensor_tensor(x[:, r, cols], x[:, r, cols], mean_var[:, 0:1], gain[:, cols],
                                             ALU.subtract, ALU.mult).then_inc(gained_done, 1)
                dve.wait_ge(rstd_done, at + 1)
                for half, cols in enumerate(halves):
                    dve.wait_ge(gained_done, 2 * at + half + 1)
                    dve.scalar_tensor_tensor(x[:, r, cols], x[:, r, cols], rstd[:, 0:1], shift[:, cols],
                                             ALU.mult, ALU.add).then_inc(x_ready, 1)

            def ffn_vector(f, t):
                n0 = FFN_UNIT[f]
                if t > 0:
                    norm(t - 1, 1)
                xT_lo_part(t, 1)
                lo_unit(n0 + 2)
                hidden_rows(f, 0, 0, 0, first=True)
                lo_unit(n0 + 3)
                with dve.Fori(0, CHUNKS // 2) as i:
                    for cc in (1, 2):
                        c = i * 2 + cc
                        hidden_rows(f, c - 1, 1, (cc - 1) % 2, first=True)
                        j = 2 * cc + 2
                        lo_part(i * 4 + (n0 + j), (n0 + j) % RAW, j % 4)
                        hidden_rows(f, c, 0, cc % 2)
                        lo_part(i * 4 + (n0 + j + 1), (n0 + j + 1) % RAW, (j + 1) % 4)
                        hT_lo_part(f, c - 1)
                hidden_rows(f, CHUNKS - 1, 1, 0)
                n0 += 2 * CHUNKS
                lo_unit(n0 + 2)
                hT_lo_part(f, CHUNKS - 1)
                for d in range(3, KF // 2 + 2):
                    lo_unit(n0 + d)
                norm(FFN_NORM[f], 0)

            def soften(m, pp):
                par = pp % 2
                dve.wait_ge(scores_done, m * PAIRS + pp + 1)
                dve.wait_ge(rel_loaded[par], 32 * (pp // 2 + 1))
                if pp >= 2:
                    dve.wait_ge(probsT_psum, pp - 1)
                    dve.wait_ge(exp_done, 4 * (pp - 1))
                for h in range(2):
                    for r, (a, b) in enumerate(SPANS):
                        j = 2 * h + r
                        dve.tensor_tensor_reduce(probs[par][:, h, a:b], SCORES[:, h, a:b],
                                                 rel[par][:, h, 0:b - a][:, ::-1], 1.0, -3.0e38, ALU.add, ALU.max,
                                                 top[:, par, j:j + 1]).then_inc(biased_done, 1)
                dve.wait_ge(biased_done, 4 * (pp + 1))
                dve.tensor_scalar(neg_top[:, par, :], top[:, par, :], -1.0, None, ALU.mult).then_inc(neg_top_done, 1)

            def normalise(m, pp):
                par = pp % 2
                dve.wait_ge(exp_done, 4 * (pp + 1))
                dve.reciprocal(inv_total[:, par, :], total[:, par, :]).then_inc(inv_done, 1)
                dve.wait_ge(inv_done, pp + 1)
                for h in range(2):
                    for r, (a, b) in enumerate(SPANS):
                        j = 2 * h + r
                        last = dve.tensor_scalar(probs[par][:, h, a:b], probs[par][:, h, a:b],
                                                 inv_total[:, par, j:j + 1], None, ALU.mult)
                last.then_inc(probs_ready, 1)

            def sticks(m, pp):
                dve.wait_ge(masked_done, 2 * pp + 2)
                for h in range(2):
                    dve.tensor_tensor_scan(stick[:, h, ::-1], stick[:, h, ::-1], restart[:, ::-1], 1.0,
                                           ALU.mult, ALU.max).then_inc(stick_done, 1)

            def break_sticks(m, pp):
                dve.wait_ge(stick_done, 2 * pp + 2)
                dve.tensor_tensor(probs[pp % 2][:, :, 0:KEYS - 1], probs[pp % 2][:, :, 0:KEYS - 1],
                                  stick[:, :, 1:KEYS], ALU.mult).then_inc(probs_ready, 1)

            def headout_lo_part(m, pp):
                dve.wait_ge(headout_hi, m * PAIRS + pp + 1)
                dve.tensor_tensor(hT_lo[:, pp, :], HEADOUT, hT_hi[:, pp, :],
                                  ALU.subtract).then_inc(headout_lo, 1)

            def mixer_vector(m, t):
                n0 = MIX_UNIT[m]
                first, second = (soften, normalise) if m % 2 == 0 else (sticks, break_sticks)
                norm(t - 1, 1)
                xT_lo_part(t, 1)
                for n in range(n0 + 2, n0 + 6):
                    lo_unit(n)
                ahead = iter(range(n0 + 6, n0 + UNITS_MIX + 1))
                for g in range(GROUPS):
                    for p in range(2):
                        pp = 2 * g + p
                        first(m, pp)
                        if p == 0 and m % 2 == 0:
                            lo_unit(next(ahead))
                        second(m, pp)
                        if p == 0 and m % 2 == 1:
                            lo_unit(next(ahead))
                        headout = (g, p) == (GROUPS - 1, 1) or (p == 0 and m % 2 == 1)
                        if headout:
                            headout_lo_part(m, pp)
                        if p == 0 or g > 0:
                            lo_unit(next(ahead))
                        if not headout:
                            headout_lo_part(m, pp)
                norm(t, 0)
                lo_unit(n0 + UNITS_MIX + 1)

            xT_lo_part(0, 0)
            lo_first()
            lo_unit(1)
            for m in range(DEPTH):
                ffn_vector(2 * m, 3 * m)
                xT_lo_part(3 * m + 1, 0)
                mixer_vector(m, 3 * m + 1)
                xT_lo_part(3 * m + 2, 0)
                ffn_vector(2 * m + 1, 3 * m + 2)
                if m < DEPTH - 1:
                    xT_lo_part(3 * m + 3, 0)
            norm(NORMS - 1, 1)

        @block.gpsimd
        def _(pool):
            def load_norm(l):
                for dst, src in ((gain, ln_g), (shift, ln_b)):
                    row = src[l // 3, l % 3:l % 3 + 1, :]
                    pool.dma_start(dst[:], row.to_broadcast([P, D])).then_inc(norm_loaded, 16)

            def norm(l, r):
                at = ROWS * l + r
                pool.wait_ge(eps_done, at + 1)
                pool.tensor_tensor(rstd[:], var_eps[:], power[:], ALU.pow).then_inc(rstd_done, 1)

            def load_rel(pp):
                for row, col in ((0, ATT_CHUNK), (ATT_CHUNK, 0)):
                    src = bass.AP(tensor=table.tensor, offset=2 * pp * 3 * P + 1 + row + col,
                                  ap=[[1, ATT_CHUNK], [3 * P, 2], [1, 2 * P - col]])
                    pool.dma_start(rel[pp % 2][row:row + ATT_CHUNK, :, col:], src).then_inc(rel_loaded[pp % 2], 16)

            pool.memset(ident[:], 0.0).then_inc(const_set, 1)
            pool.memset(ones[:], 1.0).then_inc(const_ready, 1)
            pool.dma_start(tab[:, 0:2, :], rel_bias[0:2 * P, :].rearrange("(t p) h -> p t h", p=P)).then_inc(tab_loaded, 32)
            pool.dma_start(tab[0:1, 2, :], rel_bias[2 * P:2 * P + 1, :]).then_inc(tab_loaded, 16)
            pool.wait_ge(const_set, 1)
            pool.affine_select(ident[:], ident[:], pattern=[[-1, P]], compare_op=ALU.not_equal, fill=1.0,
                               base=0, channel_multiplier=1).then_inc(const_ready, 1)
            pool.memset(power[:], -0.5).then_inc(const_ready, 1)
            pool.memset(restart[:], 0.0).then_inc(const_set, 1)
            pool.wait_ge(const_set, 2)
            for a, b in SPANS:
                pool.memset(restart[:, b - 1:b], 1.0).then_inc(const_set, 1)
            for p in range(2):
                pool.memset(rel[p][0:ATT_CHUNK, :, 0:ATT_CHUNK], MASKED).then_inc(const_set, 1)
            pool.wait_ge(const_set, 6)
            load_norm(0)
            pool.wait_ge(tab_copied, 1)
            pool.dma_start(table, tab_row[:]).then_inc(tab_stored, 16)
            pool.wait_ge(tab_stored, 16)
            load_rel(0)
            load_rel(1)
            for l in range(NORMS):
                for r in range(ROWS):
                    norm(l, r)
                if l + 1 < NORMS:
                    pool.wait_ge(x_ready, 2 * ROWS * (l + 1))
                    load_norm(l + 1)
                if l == 0:
                    for pp in range(2, PAIRS):
                        pool.wait_ge(biased_done, 4 * (pp - 1))
                        load_rel(pp)
                if l == 3:
                    for pp in range(PAIRS):
                        for k, (t, fill) in enumerate(((probs[pp % 2], 0.0), (stick, 1.0))):
                            pool.wait_ge(sigmoid_done, 2 * pp + k + 1)
                            d = t[:, :, DIAG:].rearrange("p h (b n) -> p h b n", b=2)
                            pool.affine_select(d, d, pattern=[[0, 2], [0, 2], [-1, P]], compare_op=ALU.is_gt,
                                               fill=fill, base=0, channel_multiplier=1).then_inc(masked_done, 1)


def kernel(x, w_qkv_a, w_o_a, rel_bias, w_qkv_b, w_o_b, ffn_w_gate, ffn_w_up, ffn_w_down, ln_g, ln_b):
    import numpy as np
    import concourse.bacc as bacc
    from concourse.bass_utils import run_bass_kernel_spmd

    nc = bacc.Bacc("TRN2", target_bir_lowering=False, num_devices=1)
    given = dict(x=x, w_qkv_a=w_qkv_a, w_o_a=w_o_a, rel_bias=rel_bias, w_qkv_b=w_qkv_b, w_o_b=w_o_b,
                 ffn_w_gate=ffn_w_gate, ffn_w_up=ffn_w_up, ffn_w_down=ffn_w_down, ln_g=ln_g, ln_b=ln_b)
    arrays = {"in_" + name: np.ascontiguousarray(a) for name, a in given.items()}
    t = {name[3:]: nc.dram_tensor(name, a.shape, F32, kind="ExternalInput").ap() for name, a in arrays.items()}
    table = nc.dram_tensor("bias_by_distance", (HEADS, 3 * P), F32, kind="Internal").ap()
    out = nc.dram_tensor("out", (1, SEQ, D), F32, kind="ExternalOutput").ap()
    build(nc, t["x"], (t["w_qkv_a"][0], t["w_qkv_b"][0]), (t["w_o_a"][0], t["w_o_b"][0]), t["rel_bias"],
          t["ffn_w_gate"], t["ffn_w_up"], t["ffn_w_down"], t["ln_g"], t["ln_b"], table, out)
    return run_bass_kernel_spmd(nc, [arrays], core_ids=[0]).results[0]["out"]
```

```python
from contextlib import ExitStack

import concourse.bass as bass
from concourse import mybir

F32 = mybir.dt.float32
F32R = mybir.dt.float32r
ALU = mybir.AluOpType
ACT = mybir.ActivationFunctionType
AX_X = mybir.AxisListType.X

P = 128
SEQ, D, FF, HEADS, HD = 256, 1024, 2816, 16, 64
DEPTH = 2
ROWS = SEQ // P
KD = D // P
KF = FF // P
HALF = D // 2
CHUNK_F = 256
CHUNKS = FF // CHUNK_F
CLIP = 128
ATT_CHUNK = 64
GROUP = 4
GROUPS = HEADS // GROUP
PAIRS = HEADS // 2
SCALE = HD ** -0.5
ALPHA = (2.0 * DEPTH) ** 0.25
EPS = 1e-5
MASKED = -1e30
HELD = 3

RAW = 4
SPLIT = 5
UNITS_FFN = 2 * CHUNKS + KF // 2
UNITS_MIX = 4 * GROUPS
FFN_UNIT = [0, UNITS_FFN + UNITS_MIX, 2 * UNITS_FFN + UNITS_MIX, 3 * UNITS_FFN + 2 * UNITS_MIX]
MIX_UNIT = [UNITS_FFN, 3 * UNITS_FFN + UNITS_MIX]
UNITS = 4 * UNITS_FFN + 2 * UNITS_MIX
FFN_NORM = [0, 2, 3, 5]
MIX_NORM = [1, 4]
MIX_XT = MIX_NORM
NORMS = 3 * DEPTH
NORM_UNIT = [MIX_UNIT[0], FFN_UNIT[1], FFN_UNIT[2], MIX_UNIT[1], FFN_UNIT[3], UNITS]
NORM_SCALE = [(2 * ALPHA, 4 * EPS), (ALPHA, EPS), (2 * ALPHA, 4 * EPS)] * DEPTH

FFN_SLOTS = [j % 4 for j in range(24)] + [4, 0, 1, 2, 3, 0, 4, 2, 3]
MIX_SLOTS = [0, 1, 4, 2, 3] + [4, 0, 1, 2, 3] * 2 + [4]
SLOT = (FFN_SLOTS + MIX_SLOTS + FFN_SLOTS) * DEPTH
assert len(SLOT) == UNITS and len(FFN_SLOTS) == UNITS_FFN and len(MIX_SLOTS) == UNITS_MIX


def former(n):
    return max((k for k in range(n) if SLOT[k] == SLOT[n]), default=None)


MIX_ORDER = ([("v", 0), ("v", 1), ("q", 0), ("k", 0), ("q", 1), ("k", 1)]
             + [(what, g) for g in range(2, GROUPS) for what in "vqk"] + [("o", g) for g in range(GROUPS)])
BLOCKS = [("v", 0, 0), ("v", 1, 0), ("v", 0, 1), ("v", 1, 1)]
for g in range(GROUPS):
    if g >= 2:
        BLOCKS += [("v", g, 0), ("v", g, 1)]
    BLOCKS += [(what, g, pair) for pair in range(2) for what in "qk"]
FIRST_BLOCKS = 7

AHEAD = [(6, 7), (8, 9), (10, 11), (12, 13), (14, None), (15, 16), (None, 17), (None, None)]

KEYS = 384
SPANS = [(256, 384), (0, 256)]
DIAG = 128


def build(nc, x_in, w_qkv, w_o, rel_bias, w_gate, w_up, w_down, ln_g, ln_b, table, out):
    with ExitStack() as ctx:
        def sb(name, shape, dt=F32):
            return ctx.enter_context(nc.sbuf_tensor(name, shape, dt))

        def sem(name):
            return ctx.enter_context(nc.semaphore(name))

        raw = [sb(f"raw{s}", [P, 2048]) for s in range(RAW)]
        w_hi = [sb(f"w_hi{s}", [P, 2048], F32R) for s in range(SPLIT)]
        w_lo = [sb(f"w_lo{s}", [P, 2048], F32R) for s in range(SPLIT)]
        x = sb("x", [P, ROWS, D])
        xT_hi = sb("xT_hi", [P, KD, SEQ], F32R)
        xT_lo = sb("xT_lo", [P, KD, SEQ], F32R)
        hT_at = nc.sbuf_base
        hT_hi = sb("hT_hi", [P, KF, SEQ], F32R)
        hT_lo = sb("hT_lo", [P, KF, SEQ], F32R)
        assert nc.sbuf_base - hT_at == 2 * KF * SEQ * 4
        place = [hT_at + PAIRS * SEQ * 4, hT_at + (KF + PAIRS) * SEQ * 4]
        room = [hT_at + KF * SEQ * 4, hT_at + 2 * KF * SEQ * 4]

        def in_hT(which, name, shape):
            size = 4 * shape[1] * shape[2]
            place[which] += size
            assert place[which] <= room[which]
            return nc.alloc_sbuf_tensor_at(name, shape, F32, offset=place[which] - size)

        qT = [in_hT(0, f"qT{g}", [P, 2, SEQ]) for g in range(2)]
        kT = [in_hT(0, f"kT{g}", [P, 2, SEQ]) for g in range(2)]
        v = [in_hT(0, f"v{g}", [P, ROWS, GROUP * HD]) for g in range(2)]
        probs = [in_hT(1, f"probs{p}", [P, 2, KEYS]) for p in range(2)]
        stick = in_hT(1, "stick", [P, 2, KEYS])
        probsT = in_hT(1, "probsT", [P, 2, KEYS])
        gate_act = sb("gate_act", [P, ROWS, CHUNK_F])
        hidden = sb("hidden", [P, ROWS, CHUNK_F])
        gain = sb("gain", [P, D])
        shift = sb("shift", [P, D])
        rel = [sb(f"rel{p}", [P, 2, 2 * P]) for p in range(2)]
        ident = sb("ident", [P, P])
        restart = sb("restart", [P, KEYS])
        stats = sb("stats", [P, 2, 6])
        mean_var = sb("mean_var", [P, 2])
        var_eps = sb("var_eps", [P, 1])
        rstd = sb("rstd", [P, 1])
        power = sb("power", [P, 1])
        top = sb("top", [P, 2, 4])
        neg_top = sb("neg_top", [P, 2, 4])
        total = sb("total", [P, 2, 4])
        inv_total = sb("inv_total", [P, 2, 4])
        ones = sb("ones", [1, P])
        tab = sb("tab", [P, 3, HEADS])
        tab_row = sb("tab_row", [HEADS, 3 * P])

        psum = ctx.enter_context(nc.psum_tensor("psum", [P, 8, 512], F32))
        GU = [[psum[:, 0, :], psum[:, 1, :]], [psum[:, 2, :], psum[:, 3, :]]]
        TURN = psum[:, 4, :]
        Y = [[psum[:, 5, :], psum[:, 6, :]], [psum[:, 7, :], psum[:, 3, :]]]

        def XT(t, half):
            return psum[:, 4 if half == 0 else 1 if t in MIX_XT else 2, :]

        SCORES = psum[:, 0:2, 0:KEYS]
        HEADOUT = psum[:, 4, 0:SEQ]

        def PROJ(i):
            return psum[:, 0 if i == 1 else 2 + i % 2, 0:SEQ]

        raw_loaded = [sem(f"raw_loaded{s}") for s in range(RAW)]
        hi_done, lo_done, unit_used = sem("hi_done"), sem("lo_done"), sem("unit_used")
        first_loaded, first_hi, first_lo = sem("first_loaded"), sem("first_hi"), sem("first_lo")
        x_loaded = [sem(f"x_loaded{r}") for r in range(ROWS)]
        norm_loaded = sem("norm_loaded")
        xT_psum, xT_hi_done, xT_lo_done = sem("xT_psum"), sem("xT_hi_done"), sem("xT_lo_done")
        gu_done = sem("gu_done")
        silu_done, hidden_done = sem("silu_done"), sem("hidden_done")
        hT_psum, hT_hi_done, hT_lo_done = sem("hT_psum"), sem("hT_hi_done"), sem("hT_lo_done")
        y_done = sem("y_done")
        resid_done = sem("resid_done")
        stats_done, mean_done, eps_done = sem("stats_done"), sem("mean_done"), sem("eps_done")
        rstd_done = sem("rstd_done")
        gained_done, x_ready = sem("gained_done"), sem("x_ready")
        proj_done = sem("proj_done")
        proj_copied = sem("proj_copied")
        scores_done = sem("scores_done")
        biased_done, neg_top_done, exp_done, inv_done = (sem("biased_done"), sem("neg_top_done"),
                                                         sem("exp_done"), sem("inv_done"))
        sigmoid_done, masked_done, stick_done = sem("sigmoid_done"), sem("masked_done"), sem("stick_done")
        probs_ready, probsT_psum, probsT_done = sem("probs_ready"), sem("probsT_psum"), sem("probsT_done")
        headout_done, headout_hi, headout_lo = sem("headout_done"), sem("headout_hi"), sem("headout_lo")
        rel_loaded = [sem(f"rel_loaded{p}") for p in range(2)]
        tab_loaded, tab_psum, tab_copied, tab_stored = (sem("tab_loaded"), sem("tab_psum"),
                                                        sem("tab_copied"), sem("tab_stored"))
        const_set, const_ready = sem("const_set"), sem("const_ready")
        stored = sem("stored")

        block = ctx.enter_context(nc.Block())

        def as_gu(t):
            return t[:].rearrange("p (k n) -> p k n", k=KD // 2)

        def as_qkv(t):
            return t[:].rearrange("p (k n) -> p k n", k=KD)

        def as_rows(t):
            return t[:].rearrange("p (k n) -> p k n", k=2)

        def wait_block(eng, m, i):
            what, g, b = BLOCKS[i]
            if b == 0:
                eng.wait_ge(proj_done, m * 3 * GROUPS + sum(x[2] == 0 for x in BLOCKS[:i + 1]))
            else:
                eng.wait_ge(unit_used, MIX_UNIT[m] + MIX_ORDER.index((what, g)) + 1)

        def fillers(pp):
            o = [("o", g, r, half) for g in range(GROUPS) for r in range(ROWS) for half in range(2)]
            if pp < PAIRS - 2:
                at = FIRST_BLOCKS + 3 * pp
                return (BLOCKS[at:at + 3] + o)[:3], 2
            at = 5 * (pp - (PAIRS - 2)) + 1
            return o[at:at + 5], 4

        @block.sync
        def _(sp):
            def slot_free(n):
                sp.wait_ge(lo_done, n - RAW + 1)

            def load_gate_up(f, c, n, slot, wait, khs=(0, 1)):
                for kh in khs:
                    s = (slot + kh) % RAW
                    if wait:
                        slot_free(n + kh)
                    dst = as_gu(raw[s])
                    for w, at in ((w_gate, 0), (w_up, CHUNK_F)):
                        src = w[f // 2, f % 2, kh * HALF:(kh + 1) * HALF, bass.ds(c * CHUNK_F, CHUNK_F)]
                        sp.dma_start(dst[:, :, at:at + CHUNK_F],
                                     src.rearrange("(k p) n -> p k n", p=P)).then_inc(raw_loaded[s], 16)

            def load_first():
                for part in range(2):
                    k = slice(2 * part, 2 * part + 2)
                    for w, at in ((w_gate, 0), (w_up, CHUNK_F)):
                        src = w[0, 0, 2 * part * P:(2 * part + 2) * P, 0:CHUNK_F]
                        sp.dma_start(as_gu(raw[0])[:, k, at:at + CHUNK_F], src.rearrange("(k p) n -> p k n", p=P)
                                     ).then_inc((first_loaded, raw_loaded[0])[part], 16)
                sp.dma_start(x[:, 1, :], x_in[0, P:SEQ, :]).then_inc(x_loaded[1], 16)

            def load_rows(w, k0, n):
                s = n % RAW
                slot_free(n)
                for kk in range(2):
                    sp.dma_start(as_rows(raw[s])[:, kk, :],
                                 w[(k0 + kk) * P:(k0 + kk + 1) * P, :]).then_inc(raw_loaded[s], 16)

            def load_ffn(f):
                n0 = FFN_UNIT[f]
                for c in range(2):
                    first = n0 + 2 * c == 0
                    if first:
                        load_first()
                    load_gate_up(f, c, n0 + 2 * c, n0 + 2 * c, n0 + 2 * c >= RAW, (1,) if first else (0, 1))
                with sp.Fori(1, CHUNKS // 2) as i:
                    for cc in range(2):
                        load_gate_up(f, i * 2 + cc, i * 4 + (n0 + 2 * cc), n0 + 2 * cc, wait=True)
                c = CHUNKS - 1
                load_gate_up(f, c, n0 + 2 * c, n0 + 2 * c, wait=True)
                for d in range(KF // 2):
                    load_rows(w_down[f // 2, f % 2], 2 * d, n0 + 2 * CHUNKS + d)

            def load_mixer(m):
                for u in range(UNITS_MIX):
                    n = MIX_UNIT[m] + u
                    what, g = MIX_ORDER[u]
                    if what == "o":
                        load_rows(w_o[m], 2 * g, n)
                        continue
                    s = n % RAW
                    slot_free(n)
                    at = "qkv".index(what) * D + g * GROUP * HD
                    for kh in range(2):
                        src = w_qkv[m][kh * HALF:(kh + 1) * HALF, at:at + GROUP * HD]
                        sp.dma_start(as_qkv(raw[s])[:, kh * 4:kh * 4 + 4, :],
                                     src.rearrange("(k p) n -> p k n", p=P)).then_inc(raw_loaded[s], 16)

            for m in range(DEPTH):
                load_ffn(2 * m)
                load_mixer(m)
                load_ffn(2 * m + 1)
            for r in range(ROWS):
                for half in range(2):
                    sp.wait_ge(x_ready, ((NORMS - 1) * ROWS + r) * 2 + half + 1)
                    rows, cols = slice(r * P, (r + 1) * P), slice(half * HALF, (half + 1) * HALF)
                    sp.dma_start(out[0, rows, cols], x[:, r, cols]).then_inc(stored, 16)
            sp.wait_ge(stored, 2 * 16 * ROWS)

        @block.tensor
        def _(pe):
            def unit_ready(n):
                pe.wait_ge(lo_done, n + 1)

            def transpose_x(t, r):
                for hb in range(2):
                    if t == 0:
                        pe.wait_ge(x_loaded[r], 16)
                    else:
                        pe.wait_ge(x_ready, ((t - 1) * ROWS + r) * 2 + hb + 1)
                    if r > 0:
                        pe.wait_ge(xT_lo_done, 4 * t + hb + 1)
                    for k in range(4):
                        kk = 4 * hb + k
                        last = pe.transpose(XT(t, hb)[:, k * P:(k + 1) * P], x[:, r, kk * P:(kk + 1) * P], ident[:])
                    last.then_inc(xT_psum, 1)

            def xT_ready(t, r, half):
                pe.wait_ge(xT_lo_done, 4 * t + 2 * r + half + 1)

            def three(acc, st, mv, first, last):
                pe.matmul(acc, st[0], mv[0], start=first, stop=False)
                pe.matmul(acc, st[1], mv[0], start=False, stop=False)
                return pe.matmul(acc, st[0], mv[1], start=False, stop=last)

            def static_zero(n):
                return isinstance(n, int) and n == 0

            def gate_up(r, par, slot, n, release, between=None, t=None):
                for kh in range(2):
                    s = (slot + kh) % 4
                    if not release and not (static_zero(n) and kh == 0):
                        unit_ready(n + kh)
                    if t is not None:
                        xT_ready(t, r, kh)
                    for k in range(4):
                        kk = 4 * kh + k
                        if static_zero(n) and not release and kk in (0, 2):
                            pe.wait_ge((first_lo, lo_done)[kk // 2], 1)
                        if between and kk == KD - 1:
                            between()
                        rows = slice(r * P, (r + 1) * P)
                        last = three(GU[par][r], (xT_hi[:, kk, rows], xT_lo[:, kk, rows]),
                                     (as_gu(w_hi[s])[:, k, :], as_gu(w_lo[s])[:, k, :]), kk == 0, kk == KD - 1)
                    if release and kh == 0:
                        last.then_inc(unit_used, 1)
                return last

            def turn_hidden(h_wait):
                pe.wait_ge(hidden_done, h_wait)
                for j in range(2):
                    for r in range(ROWS):
                        last = pe.transpose(TURN[:, (2 * j + r) * P:(2 * j + r + 1) * P],
                                            hidden[:, r, j * P:(j + 1) * P], ident[:])
                last.then_inc(hT_psum, 1)

            def chunk_in_loop(f, i, cc):
                n0 = FFN_UNIT[f]
                n, par, slot = i * 4 + (n0 + 2 * cc), cc % 2, 2 * cc
                gate_up(0, par, slot, n, False).then_inc(gu_done, 1)
                turn_hidden(i * 4 + (f * CHUNKS * ROWS + 2 * cc))
                gate_up(1, par, slot, n, True).then_inc(unit_used, 1)

            def half_block(r, half, d, n, count, ready=None):
                s = SLOT[n]
                rows, cols = slice(r * P, (r + 1) * P), slice(half * HALF, (half + 1) * HALF)
                for kk in range(2):
                    k = 2 * d + kk
                    if ready:
                        ready(kk)
                    last = three(Y[r][half], (hT_hi[:, k, rows], hT_lo[:, k, rows]),
                                 (as_rows(w_hi[s])[:, kk, cols], as_rows(w_lo[s])[:, kk, cols]),
                                 k == 0, k == 2 * count - 1)
                return last

            def ffn_matmul(f, t, finish):
                n0 = FFN_UNIT[f]
                gate_up(0, 0, 0, n0, False, lambda: transpose_x(t, 1), t).then_inc(gu_done, 1)
                if f == 0:
                    relative_table()
                gate_up(1, 0, 0, n0, True, t=t).then_inc(unit_used, 1)
                with pe.Fori(0, CHUNKS // 2) as i:
                    for cc in (1, 2):
                        chunk_in_loop(f, i, cc)
                n0, count = n0 + 2 * CHUNKS, KF // 2
                for d in range(count - HELD):
                    unit_ready(n0 + d)
                    if d == 0:
                        pe.wait_ge(hidden_done, (f * CHUNKS + CHUNKS - 1) * ROWS)
                    if d == 1:
                        turn_hidden((f + 1) * CHUNKS * ROWS)
                    pe.wait_ge(hT_lo_done, f * CHUNKS + d + 1)
                    for r in range(ROWS):
                        for half in range(2):
                            last = half_block(r, half, d, n0 + d, count)
                    last.then_inc(unit_used, 1)
                pe.wait_ge(hT_lo_done, (f + 1) * CHUNKS)
                for r in range(ROWS):
                    for half in range(2):
                        for d in range(count - HELD, count):
                            if r == 0 and half == 0:
                                unit_ready(n0 + d)
                            if r == 1 and half == 1 and d == count - 1:
                                finish()
                            last = half_block(r, half, d, n0 + d, count)
                            if r == 1 and half == 1:
                                last.then_inc(unit_used, 1)
                        if not (r == 1 and half == 1):
                            last.then_inc(y_done, 1)

            def proj_block(m, i, t=None):
                what, g, b = BLOCKS[i]
                n = MIX_UNIT[m] + MIX_ORDER.index((what, g))
                hi, lo = as_qkv(w_hi[SLOT[n]]), as_qkv(w_lo[SLOT[n]])
                if b == 0:
                    unit_ready(n)
                if i >= 2:
                    pe.wait_ge(proj_copied, m * len(BLOCKS) + i - 1)
                acc = PROJ(i)
                part = slice(b * P, (b + 1) * P)
                for k in range(KD):
                    if t is not None and k % 4 == 0:
                        xT_ready(t, b, k // 4)
                    if what == "v":
                        last = three(acc, (xT_hi[:, k, part], xT_lo[:, k, part]), (hi[:, k, :], lo[:, k, :]),
                                     k == 0, k == KD - 1)
                    else:
                        last = three(acc, (hi[:, k, part], lo[:, k, part]), (xT_hi[:, k, :], xT_lo[:, k, :]),
                                     k == 0, k == KD - 1)
                last.then_inc(proj_done if b == 0 else unit_used, 1)

            def out_half(m, g, r, half):
                n = MIX_UNIT[m] + 3 * GROUPS + g
                if half == 0:
                    unit_ready(n)
                if (g, r, half) == (0, 1, 1):
                    pe.wait_ge(proj_copied, (m + 1) * len(BLOCKS))
                last = half_block(r, half, g, n, GROUPS,
                                  lambda kk: pe.wait_ge(headout_lo, m * PAIRS + 2 * g + kk + 1))
                if (r, half) == (1, 1):
                    last.then_inc(unit_used, 1)
                elif g == GROUPS - 1:
                    last.then_inc(y_done, 1)

            def scores(m, pp):
                g, p = pp // 2, pp % 2
                pe.wait_ge(proj_copied, m * len(BLOCKS) + BLOCKS.index(("k", g, p)) + 1)
                if m * PAIRS + pp > 0:
                    pe.wait_ge(probsT_done, m * PAIRS + pp)
                q, k = qT[g % 2], kT[g % 2]
                for h in range(2):
                    part = slice(h * HD, (h + 1) * HD)
                    for r, (a, b) in enumerate(SPANS):
                        last = pe.matmul(SCORES[:, h, a:b], q[part, p, r * P:(r + 1) * P], k[part, p, 0:b - a],
                                         start=True, stop=True)
                last.then_inc(scores_done, 1)

            def turn_probs(m, pp):
                pe.wait_ge(probs_ready, m * PAIRS + pp + 1)
                pr = probs[pp % 2]
                for h in range(2):
                    for to, at in ((0, 2 * P), (P, 0), (2 * P, P)):
                        last = pe.transpose(SCORES[:, h, to:to + P], pr[:, h, at:at + P], ident[:])
                last.then_inc(probsT_psum, 1)

            def head_out(m, pp):
                g, p = pp // 2, pp % 2
                pe.wait_ge(probsT_done, m * PAIRS + pp + 1)
                if m * PAIRS + pp > 0:
                    pe.wait_ge(headout_lo, m * PAIRS + pp)
                for h in range(2):
                    acc = HEADOUT[h * HD:(h + 1) * HD, :]
                    cols = slice((2 * p + h) * HD, (2 * p + h + 1) * HD)
                    pe.matmul(acc, v[g % 2][:, 0, cols], probsT[:, h, 0:2 * P], start=True, stop=False)
                    last = pe.matmul(acc[:, P:2 * P], v[g % 2][:, 1, cols], probsT[:, h, 2 * P:3 * P],
                                     start=False, stop=True)
                last.then_inc(headout_done, 1)

            def mixer_matmul(m, t, finish):
                proj_block(m, 0, t=t)
                proj_block(m, 1)
                transpose_x(t, 1)
                proj_block(m, 2, t=t)
                for i in range(3, FIRST_BLOCKS):
                    proj_block(m, i)
                for pp in range(PAIRS):
                    scores(m, pp)
                    todo, turn = fillers(pp)
                    for j, block in enumerate(todo):
                        if j == turn:
                            turn_probs(m, pp)
                        if block[0] == "o":
                            out_half(m, *block[1:])
                        else:
                            proj_block(m, BLOCKS.index(block))
                    head_out(m, pp)
                last_g = GROUPS - 1
                for half in range(2):
                    out_half(m, last_g, 0, half)
                out_half(m, last_g - 1, 1, 1)
                out_half(m, last_g, 1, 0)
                finish()
                out_half(m, last_g, 1, 1)

            def relative_table():
                pe.wait_ge(tab_loaded, 48)
                pe.matmul(Y[0][0][0:HEADS, 0:P], tab[:, 0, :], ident[:], start=True, stop=True)
                pe.matmul(Y[0][0][0:HEADS, P:2 * P], tab[:, 1, :], ident[:], start=True, stop=True)
                pe.matmul(Y[0][0][0:HEADS, 2 * P:3 * P], tab[0:1, 2, :], ones[:], start=True,
                          stop=True).then_inc(tab_psum, 1)

            pe.wait_ge(const_ready, 2)
            transpose_x(0, 0)
            for m in range(DEPTH):
                t = 3 * m
                ffn_matmul(2 * m, t, lambda: transpose_x(t + 1, 0))
                mixer_matmul(m, t + 1, lambda: transpose_x(t + 2, 0))
                ffn_matmul(2 * m + 1, t + 2, lambda: transpose_x(t + 3, 0) if m < DEPTH - 1 else None)

        @block.scalar
        def _(act):
            def hi_part(n, raw_slot, count, slot, before):
                act.wait_ge(raw_loaded[raw_slot], count * 32)
                if before is not None:
                    act.wait_ge(unit_used, before + 1)
                act.activation(w_hi[slot][:], raw[raw_slot][:], ACT.Copy).then_inc(hi_done, 1)

            def hi_unit(n):
                if n < UNITS:
                    hi_part(n, n % RAW, n // RAW + 1, SLOT[n], former(n))

            def hi_first():
                for part in range(2):
                    act.wait_ge((first_loaded, raw_loaded[0])[part], 32)
                    cols = slice(1024 * part, 1024 * part + 1024)
                    act.activation(w_hi[0][:, cols], raw[0][:, cols], ACT.Copy).then_inc((first_hi, hi_done)[part], 1)

            def silu(f, c, r, par, again=True):
                idx = c * 2 + (f * CHUNKS * ROWS + r)
                if r == 0:
                    act.wait_ge(gu_done, c + (f * CHUNKS + 1))
                else:
                    act.wait_ge(unit_used, c * 2 + (FFN_UNIT[f] + 2))
                if r == 0 and again:
                    act.wait_ge(hidden_done, idx - 1)
                act.activation(gate_act[:, r, :], GU[par][r][:, 0:CHUNK_F], ACT.Silu).then_inc(silu_done, 1)

            def hT_hi_part(f, c):
                act.wait_ge(hT_psum, c + (f * CHUNKS + 1))
                act.activation(hT_hi[:, bass.ds(c * 2, 2), :], TURN.rearrange("p (k n) -> p k n", k=2),
                               ACT.Copy).then_inc(hT_hi_done, 1)

            def xT_hi_part(t, r):
                for hb in range(2):
                    act.wait_ge(xT_psum, 4 * t + 2 * r + hb + 1)
                    act.activation(xT_hi[:, 4 * hb:4 * hb + 4, r * P:(r + 1) * P],
                                   XT(t, hb).rearrange("p (k n) -> p k n", k=4), ACT.Copy).then_inc(xT_hi_done, 1)

            def ffn_scalar(f, t):
                n0 = FFN_UNIT[f]
                xT_hi_part(t, 1)
                hi_unit(n0 + 2)
                silu(f, 0, 0, 0, again=False)
                if f == 0:
                    relative_table()
                hi_unit(n0 + 3)
                with act.Fori(0, CHUNKS // 2) as i:
                    for cc in (1, 2):
                        c = i * 2 + cc
                        silu(f, c - 1, 1, (cc - 1) % 2)
                        for kh in range(2):
                            j = 2 * cc + 2 + kh
                            n = n0 + j
                            hi_part(i * 4 + n, n % RAW, i + (n // RAW + 1), j % 4, i * 4 + (n - 4))
                        silu(f, c, 0, cc % 2)
                        hT_hi_part(f, c - 1)
                silu(f, CHUNKS - 1, 1, 0)
                n0 += 2 * CHUNKS
                hi_unit(n0 + 2)
                hT_hi_part(f, CHUNKS - 1)
                for d in range(3, KF // 2 + 2):
                    hi_unit(n0 + d)

            def copy_proj(m, i):
                what, g, b = BLOCKS[i]
                wait_block(act, m, i)
                if g >= 2:
                    act.wait_ge(headout_done, m * PAIRS + 2 * (g - 1))
                dst = {"v": v, "q": qT, "k": kT}[what][g % 2]
                act.activation(dst[:, b, :], PROJ(i), ACT.Copy,
                               scale=SCALE if what == "q" else 1.0).then_inc(proj_copied, 1)

            def exps(m, pp):
                par = pp % 2
                act.wait_ge(neg_top_done, m * PAIRS + pp + 1)
                for h in range(2):
                    for r, (a, b) in enumerate(SPANS):
                        j = 2 * h + r
                        act.activation(probs[par][:, h, a:b], probs[par][:, h, a:b], ACT.Exp,
                                       bias=neg_top[:, par, j:j + 1],
                                       accum_out=total[:, par, j:j + 1]).then_inc(exp_done, 1)

            def sigmoids(m, pp):
                act.wait_ge(scores_done, m * PAIRS + pp + 1)
                if pp >= 2:
                    act.wait_ge(probsT_psum, m * PAIRS + pp - 1)
                act.activation(probs[pp % 2][:], SCORES, ACT.Sigmoid).then_inc(sigmoid_done, 1)
                if pp >= 1:
                    act.wait_ge(probs_ready, m * PAIRS + pp)
                act.activation(stick[:], SCORES, ACT.Sigmoid, scale=-1.0).then_inc(sigmoid_done, 1)

            def probsT_copy(m, pp):
                act.wait_ge(probsT_psum, m * PAIRS + pp + 1)
                if m * PAIRS + pp > 0:
                    act.wait_ge(headout_done, m * PAIRS + pp)
                act.activation(probsT[:], SCORES, ACT.Copy).then_inc(probsT_done, 1)

            def headout_hi_part(m, pp):
                act.wait_ge(headout_done, m * PAIRS + pp + 1)
                act.activation(hT_hi[:, pp, :], HEADOUT, ACT.Copy).then_inc(headout_hi, 1)

            def mixer_scalar(m, t):
                n0 = MIX_UNIT[m]
                weights = exps if m % 2 == 0 else sigmoids
                hi_unit(n0 + 2)
                copy_proj(m, 0)
                copy_proj(m, 1)
                xT_hi_part(t, 1)
                hi_unit(n0 + 3)
                copy_proj(m, 2)
                copy_proj(m, 3)
                hi_unit(n0 + 4)
                for i in range(4, FIRST_BLOCKS):
                    copy_proj(m, i)
                hi_unit(n0 + 5)
                for pp in range(PAIRS):
                    blocks = [BLOCKS.index(todo) for todo in fillers(pp)[0] if todo[0] != "o"]
                    during, after = AHEAD[pp]
                    weights(m, pp)
                    for j, i in enumerate(blocks[0:2]):
                        copy_proj(m, i)
                        if j == 0 and during:
                            hi_unit(n0 + during)
                    probsT_copy(m, pp)
                    if after:
                        hi_unit(n0 + after)
                    for i in blocks[2:]:
                        copy_proj(m, i)
                    headout_hi_part(m, pp)

            def relative_table():
                act.wait_ge(tab_psum, 1)
                act.activation(tab_row[:], Y[0][0][0:HEADS, 0:3 * P], ACT.Copy).then_inc(tab_copied, 1)

            act.dma_start(x[:, 0, :], x_in[0, 0:P, :]).then_inc(x_loaded[0], 16)
            xT_hi_part(0, 0)
            hi_first()
            hi_unit(1)
            for m in range(DEPTH):
                ffn_scalar(2 * m, 3 * m)
                xT_hi_part(3 * m + 1, 0)
                mixer_scalar(m, 3 * m + 1)
                xT_hi_part(3 * m + 2, 0)
                ffn_scalar(2 * m + 1, 3 * m + 2)
                if m < DEPTH - 1:
                    xT_hi_part(3 * m + 3, 0)

        @block.vector
        def _(dve):
            def lo_part(n, raw_slot, slot):
                dve.wait_ge(hi_done, n + 1)
                dve.tensor_tensor(w_lo[slot][:], raw[raw_slot][:], w_hi[slot][:], ALU.subtract).then_inc(lo_done, 1)

            def lo_unit(n):
                if n < UNITS:
                    lo_part(n, n % RAW, SLOT[n])

            def lo_first():
                for part in range(2):
                    dve.wait_ge((first_hi, hi_done)[part], 1)
                    cols = slice(1024 * part, 1024 * part + 1024)
                    last = dve.tensor_tensor(w_lo[0][:, cols], raw[0][:, cols], w_hi[0][:, cols], ALU.subtract)
                    last.then_inc((first_lo, lo_done)[part], 1)

            def hidden_rows(f, c, r, par, first=False):
                idx = c * 2 + (f * CHUNKS * ROWS + r)
                dve.wait_ge(silu_done, idx + 1)
                if not first:
                    dve.wait_ge(hT_psum, c + f * CHUNKS)
                dve.tensor_tensor(hidden[:, r, :], GU[par][r][:, CHUNK_F:], gate_act[:, r, :],
                                  ALU.mult).then_inc(hidden_done, 1)

            def hT_lo_part(f, c):
                dve.wait_ge(hT_hi_done, c + (f * CHUNKS + 1))
                dve.tensor_tensor(hT_lo[:, bass.ds(c * 2, 2), :], TURN.rearrange("p (k n) -> p k n", k=2),
                                  hT_hi[:, bass.ds(c * 2, 2), :], ALU.subtract).then_inc(hT_lo_done, 1)

            def xT_lo_part(t, r):
                for hb in range(2):
                    dve.wait_ge(xT_hi_done, 4 * t + 2 * r + hb + 1)
                    dst = (slice(None), slice(4 * hb, 4 * hb + 4), slice(r * P, (r + 1) * P))
                    dve.tensor_tensor(xT_lo[dst], XT(t, hb).rearrange("p (k n) -> p k n", k=4), xT_hi[dst],
                                      ALU.subtract).then_inc(xT_lo_done, 1)

            def norm(l, r):
                scale, eps = NORM_SCALE[l]
                at = ROWS * l + r
                halves = [slice(half * HALF, (half + 1) * HALF) for half in range(2)]
                for half, cols in enumerate(halves):
                    if r == 1 and half == 1:
                        dve.wait_ge(unit_used, NORM_UNIT[l])
                    else:
                        dve.wait_ge(y_done, 3 * l + 2 * r + half + 1)
                    dve.scalar_tensor_tensor(x[:, r, cols], x[:, r, cols], scale, Y[r][half],
                                             ALU.mult, ALU.add).then_inc(resid_done, 1)
                    dve.wait_ge(resid_done, 2 * at + half + 1)
                    dve.bn_stats(stats[:, half, :], x[:, r, cols]).then_inc(stats_done, 1)
                dve.wait_ge(stats_done, 2 * at + 2)
                dve.bn_aggr(mean_var[:], stats[:].rearrange("p a b -> p (a b)")).then_inc(mean_done, 1)
                dve.wait_ge(mean_done, at + 1)
                dve.tensor_scalar(var_eps[:], mean_var[:, 1:2], eps, None, ALU.add).then_inc(eps_done, 1)
                dve.wait_ge(norm_loaded, 32 * (l + 1))
                for half, cols in enumerate(halves):
                    dve.scalar_tensor_tensor(x[:, r, cols], x[:, r, cols], mean_var[:, 0:1], gain[:, cols],
                                             ALU.subtract, ALU.mult).then_inc(gained_done, 1)
                    if half == 0:
                        dve.wait_ge(rstd_done, at + 1)
                    dve.wait_ge(gained_done, 2 * at + half + 1)
                    dve.scalar_tensor_tensor(x[:, r, cols], x[:, r, cols], rstd[:, 0:1], shift[:, cols],
                                             ALU.mult, ALU.add).then_inc(x_ready, 1)

            def ffn_vector(f, t):
                n0 = FFN_UNIT[f]
                if t > 0:
                    norm(t - 1, 1)
                xT_lo_part(t, 1)
                lo_unit(n0 + 2)
                hidden_rows(f, 0, 0, 0, first=True)
                lo_unit(n0 + 3)
                with dve.Fori(0, CHUNKS // 2) as i:
                    for cc in (1, 2):
                        c = i * 2 + cc
                        hidden_rows(f, c - 1, 1, (cc - 1) % 2, first=True)
                        j = 2 * cc + 2
                        lo_part(i * 4 + (n0 + j), (n0 + j) % RAW, j % 4)
                        hidden_rows(f, c, 0, cc % 2)
                        lo_part(i * 4 + (n0 + j + 1), (n0 + j + 1) % RAW, (j + 1) % 4)
                        hT_lo_part(f, c - 1)
                hidden_rows(f, CHUNKS - 1, 1, 0)
                n0 += 2 * CHUNKS
                lo_unit(n0 + 2)
                hT_lo_part(f, CHUNKS - 1)
                for d in range(3, KF // 2 + 2):
                    lo_unit(n0 + d)
                norm(FFN_NORM[f], 0)

            def soften(m, pp):
                par = pp % 2
                dve.wait_ge(scores_done, m * PAIRS + pp + 1)
                dve.wait_ge(rel_loaded[par], 32 * (pp // 2 + 1))
                if pp >= 2:
                    dve.wait_ge(probsT_psum, pp - 1)
                    dve.wait_ge(exp_done, 4 * (pp - 1))
                for h in range(2):
                    for r, (a, b) in enumerate(SPANS):
                        j = 2 * h + r
                        dve.tensor_tensor_reduce(probs[par][:, h, a:b], SCORES[:, h, a:b],
                                                 rel[par][:, h, 0:b - a][:, ::-1], 1.0, -3.0e38, ALU.add, ALU.max,
                                                 top[:, par, j:j + 1]).then_inc(biased_done, 1)
                dve.wait_ge(biased_done, 4 * (pp + 1))
                dve.tensor_scalar(neg_top[:, par, :], top[:, par, :], -1.0, None, ALU.mult).then_inc(neg_top_done, 1)

            def normalise(m, pp):
                par = pp % 2
                dve.wait_ge(exp_done, 4 * (pp + 1))
                dve.reciprocal(inv_total[:, par, :], total[:, par, :]).then_inc(inv_done, 1)
                dve.wait_ge(inv_done, pp + 1)
                for h in range(2):
                    for r, (a, b) in enumerate(SPANS):
                        j = 2 * h + r
                        last = dve.tensor_scalar(probs[par][:, h, a:b], probs[par][:, h, a:b],
                                                 inv_total[:, par, j:j + 1], None, ALU.mult)
                last.then_inc(probs_ready, 1)

            def sticks(m, pp):
                dve.wait_ge(masked_done, 2 * pp + 2)
                for h in range(2):
                    dve.tensor_tensor_scan(stick[:, h, ::-1], stick[:, h, ::-1], restart[:, ::-1], 1.0,
                                           ALU.mult, ALU.max).then_inc(stick_done, 1)

            def break_sticks(m, pp):
                dve.wait_ge(stick_done, 2 * pp + 2)
                dve.tensor_tensor(probs[pp % 2][:, :, 0:KEYS - 1], probs[pp % 2][:, :, 0:KEYS - 1],
                                  stick[:, :, 1:KEYS], ALU.mult).then_inc(probs_ready, 1)

            def headout_lo_part(m, pp):
                dve.wait_ge(headout_hi, m * PAIRS + pp + 1)
                dve.tensor_tensor(hT_lo[:, pp, :], HEADOUT, hT_hi[:, pp, :],
                                  ALU.subtract).then_inc(headout_lo, 1)

            def mixer_vector(m, t):
                n0 = MIX_UNIT[m]
                norm(t - 1, 1)
                xT_lo_part(t, 1)
                for n in range(n0 + 2, n0 + 5):
                    lo_unit(n)
                before = 5
                for pp in range(PAIRS):
                    if m % 2 == 0:
                        soften(m, pp)
                    if before and pp < PAIRS - 1:
                        lo_unit(n0 + before)
                    if m % 2 == 0:
                        normalise(m, pp)
                    else:
                        sticks(m, pp)
                        break_sticks(m, pp)
                    during = AHEAD[pp][0] if pp < PAIRS - 1 else before
                    if during:
                        lo_unit(n0 + during)
                    headout_lo_part(m, pp)
                    before = AHEAD[pp][1]
                norm(t, 0)

            xT_lo_part(0, 0)
            lo_first()
            lo_unit(1)
            for m in range(DEPTH):
                ffn_vector(2 * m, 3 * m)
                xT_lo_part(3 * m + 1, 0)
                mixer_vector(m, 3 * m + 1)
                xT_lo_part(3 * m + 2, 0)
                ffn_vector(2 * m + 1, 3 * m + 2)
                if m < DEPTH - 1:
                    xT_lo_part(3 * m + 3, 0)
            norm(NORMS - 1, 1)

        @block.gpsimd
        def _(pool):
            def load_norm(l):
                for dst, src in ((gain, ln_g), (shift, ln_b)):
                    row = src[l // 3, l % 3:l % 3 + 1, :]
                    pool.dma_start(dst[:], row.to_broadcast([P, D])).then_inc(norm_loaded, 16)

            def norm(l, r):
                at = ROWS * l + r
                pool.wait_ge(eps_done, at + 1)
                pool.tensor_tensor(rstd[:], var_eps[:], power[:], ALU.pow).then_inc(rstd_done, 1)

            def load_rel(pp):
                for row, col in ((0, ATT_CHUNK), (ATT_CHUNK, 0)):
                    src = bass.AP(tensor=table.tensor, offset=2 * pp * 3 * P + 1 + row + col,
                                  ap=[[1, ATT_CHUNK], [3 * P, 2], [1, 2 * P - col]])
                    pool.dma_start(rel[pp % 2][row:row + ATT_CHUNK, :, col:], src).then_inc(rel_loaded[pp % 2], 16)

            pool.memset(ident[:], 0.0).then_inc(const_set, 1)
            pool.memset(ones[:], 1.0).then_inc(const_ready, 1)
            pool.dma_start(tab[:, 0:2, :], rel_bias[0:2 * P, :].rearrange("(t p) h -> p t h", p=P)).then_inc(tab_loaded, 32)
            pool.dma_start(tab[0:1, 2, :], rel_bias[2 * P:2 * P + 1, :]).then_inc(tab_loaded, 16)
            pool.wait_ge(const_set, 1)
            pool.affine_select(ident[:], ident[:], pattern=[[-1, P]], compare_op=ALU.not_equal, fill=1.0,
                               base=0, channel_multiplier=1).then_inc(const_ready, 1)
            pool.memset(power[:], -0.5).then_inc(const_ready, 1)
            pool.memset(restart[:], 0.0).then_inc(const_set, 1)
            pool.wait_ge(const_set, 2)
            for a, b in SPANS:
                pool.memset(restart[:, b - 1:b], 1.0).then_inc(const_set, 1)
            for p in range(2):
                pool.memset(rel[p][0:ATT_CHUNK, :, 0:ATT_CHUNK], MASKED).then_inc(const_set, 1)
            pool.wait_ge(const_set, 6)
            load_norm(0)
            pool.wait_ge(tab_copied, 1)
            pool.dma_start(table, tab_row[:]).then_inc(tab_stored, 16)
            pool.wait_ge(tab_stored, 16)
            load_rel(0)
            load_rel(1)
            for l in range(NORMS):
                for r in range(ROWS):
                    norm(l, r)
                if l + 1 < NORMS:
                    pool.wait_ge(x_ready, 2 * ROWS * (l + 1))
                    load_norm(l + 1)
                if l == 0:
                    for pp in range(2, PAIRS):
                        pool.wait_ge(biased_done, 4 * (pp - 1))
                        load_rel(pp)
                if l == 3:
                    for pp in range(PAIRS):
                        for k, (t, fill) in enumerate(((probs[pp % 2], 0.0), (stick, 1.0))):
                            pool.wait_ge(sigmoid_done, 2 * pp + k + 1)
                            d = t[:, :, DIAG:].rearrange("p h (b n) -> p h b n", b=2)
                            pool.affine_select(d, d, pattern=[[0, 2], [0, 2], [-1, P]], compare_op=ALU.is_gt,
                                               fill=fill, base=0, channel_multiplier=1).then_inc(masked_done, 1)


def kernel(x, w_qkv_a, w_o_a, rel_bias, w_qkv_b, w_o_b, ffn_w_gate, ffn_w_up, ffn_w_down, ln_g, ln_b):
    import numpy as np
    import concourse.bacc as bacc
    from concourse.bass_utils import run_bass_kernel_spmd

    nc = bacc.Bacc("TRN2", target_bir_lowering=False, num_devices=1)
    given = dict(x=x, w_qkv_a=w_qkv_a, w_o_a=w_o_a, rel_bias=rel_bias, w_qkv_b=w_qkv_b, w_o_b=w_o_b,
                 ffn_w_gate=ffn_w_gate, ffn_w_up=ffn_w_up, ffn_w_down=ffn_w_down, ln_g=ln_g, ln_b=ln_b)
    arrays = {"in_" + name: np.ascontiguousarray(a) for name, a in given.items()}
    t = {name[3:]: nc.dram_tensor(name, a.shape, F32, kind="ExternalInput").ap() for name, a in arrays.items()}
    table = nc.dram_tensor("bias_by_distance", (HEADS, 3 * P), F32, kind="Internal").ap()
    out = nc.dram_tensor("out", (1, SEQ, D), F32, kind="ExternalOutput").ap()
    build(nc, t["x"], (t["w_qkv_a"][0], t["w_qkv_b"][0]), (t["w_o_a"][0], t["w_o_b"][0]), t["rel_bias"],
          t["ffn_w_gate"], t["ffn_w_up"], t["ffn_w_down"], t["ln_g"], t["ln_b"], table, out)
    return run_bass_kernel_spmd(nc, [arrays], core_ids=[0]).results[0]["out"]
```

```python
from contextlib import ExitStack

import concourse.bass as bass
from concourse import mybir

F32 = mybir.dt.float32
F32R = mybir.dt.float32r
ALU = mybir.AluOpType
ACT = mybir.ActivationFunctionType

P = 128
SEQ, D, FF, HEADS, HD = 256, 1024, 2816, 16, 64
DEPTH = 2
ROWS = SEQ // P
KD = D // P
KF = FF // P
HALF = D // 2
CHUNK_F = 256
CHUNKS = FF // CHUNK_F
CLIP = 128
ATT_CHUNK = 64
GROUP = 4
GROUPS = HEADS // GROUP
PAIRS = HEADS // 2
SCALE = HD ** -0.5
ALPHA = (2.0 * DEPTH) ** 0.25
EPS = 1e-5
MASKED = 1e30
EARLY = [(0, 0, 1), (0, 1, 2), (0, 2, 3), (0, 3, 4), (1, 0, 2), (1, 2, 4)]
WARM_UP = [6, 1, 1]
FIRST_TURNS = [(3, 0), (3, 1)]
FFN_TURNS = [(6, 0), (7, 1)]
LATE_TURNS = [(7, 0), (7, 1)]
MIX_TURNS = [(3, 0), (5, 1)]
HELD = 3

RAW = 4
SPLIT = 5
UNITS_FFN = 2 * CHUNKS + KF // 2
UNITS_MIX = 4 * GROUPS
FFN_UNIT = [0, UNITS_FFN + UNITS_MIX, 2 * UNITS_FFN + UNITS_MIX, 3 * UNITS_FFN + 2 * UNITS_MIX]
MIX_UNIT = [UNITS_FFN, 3 * UNITS_FFN + UNITS_MIX]
UNITS = 4 * UNITS_FFN + 2 * UNITS_MIX
FFN_NORM = [0, 2, 3, 5]
PIECES = [(0, 2), (2, 4), (4, 8)]
PARTS = len(PIECES)
NORMS = 3 * DEPTH
NORM_UNIT = [MIX_UNIT[0], FFN_UNIT[1], FFN_UNIT[2], MIX_UNIT[1], FFN_UNIT[3], UNITS]
NORM_SCALE = [(2 * ALPHA, 4 * EPS), (ALPHA, EPS), (2 * ALPHA, 4 * EPS)] * DEPTH

FFN_SLOTS = [j % 4 for j in range(24)] + [4, 0, 1, 2, 3, 0, 4, 2, 3]
MIX_SLOTS = [0, 1, 4, 2, 3] + [4, 0, 1, 2, 3] * 2 + [4]
SLOT = (FFN_SLOTS + MIX_SLOTS + FFN_SLOTS) * DEPTH
assert len(SLOT) == UNITS and len(FFN_SLOTS) == UNITS_FFN and len(MIX_SLOTS) == UNITS_MIX


def former(n):
    return max((k for k in range(n) if SLOT[k] == SLOT[n]), default=None)


MIX_ORDER = ([("v", 0), ("v", 1), ("q", 0), ("k", 0), ("q", 1), ("k", 1)]
             + [(what, g) for g in range(2, GROUPS) for what in "vqk"] + [("o", g) for g in range(GROUPS)])
BLOCKS = [("v", 0, 0), ("v", 1, 0), ("v", 0, 1), ("v", 1, 1)]
for group in range(GROUPS):
    if group >= 2:
        BLOCKS += [("v", group, 0), ("v", group, 1)]
    BLOCKS += [(what, group, pair) for pair in range(2) for what in "qk"]
FIRST_BLOCKS = 7

AHEAD = [(6, 7), (8, 9), (10, 11), (12, 13), (14, None), (15, 16), (None, 17), (None, None)]

KEYS = 384
SPANS = [(256, 384), (0, 256)]
DIAG = 128


def build(nc, x_in, w_qkv, w_o, rel_bias, w_gate, w_up, w_down, ln_g, ln_b, table, out):
    with ExitStack() as ctx:
        def sb(name, shape, dt=F32):
            return ctx.enter_context(nc.sbuf_tensor(name, shape, dt))

        def sem(name):
            return ctx.enter_context(nc.semaphore(name))

        raw = [sb(f"raw{s}", [P, 2048]) for s in range(RAW)]
        w_hi = [sb(f"w_hi{s}", [P, 2048], F32R) for s in range(SPLIT)]
        w_lo = [sb(f"w_lo{s}", [P, 2048], F32R) for s in range(SPLIT)]
        x = sb("x", [P, ROWS, D])
        xT_hi = sb("xT_hi", [P, KD, SEQ], F32R)
        xT_lo = sb("xT_lo", [P, KD, SEQ], F32R)
        hT_at = nc.sbuf_base
        hT_hi = sb("hT_hi", [P, KF, SEQ], F32R)
        hT_lo = sb("hT_lo", [P, KF, SEQ], F32R)
        assert nc.sbuf_base - hT_at == 2 * KF * SEQ * 4
        place = [hT_at + PAIRS * SEQ * 4, hT_at + (KF + PAIRS) * SEQ * 4]
        room = [hT_at + KF * SEQ * 4, hT_at + 2 * KF * SEQ * 4]

        def in_hT(which, name, shape):
            size = 4 * shape[1] * shape[2]
            place[which] += size
            assert place[which] <= room[which]
            return nc.alloc_sbuf_tensor_at(name, shape, F32, offset=place[which] - size)

        qT = [in_hT(0, f"qT{g}", [P, 2, SEQ]) for g in range(2)]
        kT = [in_hT(0, f"kT{g}", [P, 2, SEQ]) for g in range(2)]
        v = [in_hT(0, f"v{g}", [P, ROWS, GROUP * HD]) for g in range(2)]
        probs = [in_hT(1, f"probs{p}", [P, 2, KEYS]) for p in range(2)]
        stick = in_hT(1, "stick", [P, 2, KEYS])
        probsT = in_hT(1, "probsT", [P, 2, KEYS])
        gate_act = sb("gate_act", [P, ROWS, CHUNK_F])
        hidden = sb("hidden", [P, ROWS, CHUNK_F])
        gain = sb("gain", [P, D])
        shift = sb("shift", [P, D])
        rel = [sb(f"rel{p}", [P, 2, 2 * P]) for p in range(2)]
        ident = sb("ident", [P, P])
        restart = sb("restart", [P, KEYS])
        stats = sb("stats", [P, 2, 6])
        mean_var = sb("mean_var", [P, 2])
        var_eps = sb("var_eps", [P, 1])
        rstd = sb("rstd", [P, 1])
        power = sb("power", [P, 1])
        unread = sb("unread", [P, 1])
        neg_top = sb("neg_top", [P, 2, 4])
        total = sb("total", [P, 2, 4])
        inv_total = sb("inv_total", [P, 2, 4])
        ones = sb("ones", [1, P])
        tab = sb("tab", [P, 3, HEADS])
        tab_row = sb("tab_row", [HEADS, 3 * P])

        psum = ctx.enter_context(nc.psum_tensor("psum", [P, 8, 512], F32))
        GU = [[psum[:, 0, :], psum[:, 1, :]], [psum[:, 2, :], psum[:, 3, :]]]
        TURN = psum[:, 4, :]
        Y = [[psum[:, 5, :], psum[:, 6, :]], [psum[:, 7, :], psum[:, 3, :]]]

        def XT(piece):
            a, b = PIECES[piece]
            return psum[:, 4 + piece, 0:(b - a) * P]

        SCORES = psum[:, 0:2, 0:KEYS]
        HEADOUT = psum[:, 4, 0:SEQ]

        def PROJ(i):
            return psum[:, 0 if i == 1 else 2 + i % 2, 0:SEQ]

        raw_loaded = [sem(f"raw_loaded{s}") for s in range(RAW)]
        hi_done, lo_done, unit_used = sem("hi_done"), sem("lo_done"), sem("unit_used")
        early_loaded = [sem(f"early_loaded{n}") for n in range(2)]
        early_hi, early_lo = sem("early_hi"), sem("early_lo")
        x_loaded = [sem(f"x_loaded{i}") for i in range(3)]
        norm_loaded = sem("norm_loaded")
        xT_psum, xT_hi_done, xT_lo_done = sem("xT_psum"), sem("xT_hi_done"), sem("xT_lo_done")
        gu_done = sem("gu_done")
        silu_done, hidden_done = sem("silu_done"), sem("hidden_done")
        hT_psum, hT_hi_done, hT_lo_done = sem("hT_psum"), sem("hT_hi_done"), sem("hT_lo_done")
        y_done = sem("y_done")
        resid_done = sem("resid_done")
        stats_done, mean_done, eps_done = sem("stats_done"), sem("mean_done"), sem("eps_done")
        rstd_done = sem("rstd_done")
        gained_done, x_ready = sem("gained_done"), sem("x_ready")
        proj_done = sem("proj_done")
        proj_copied = sem("proj_copied")
        scores_done = sem("scores_done")
        biased_done, exp_done, inv_done = sem("biased_done"), sem("exp_done"), sem("inv_done")
        sigmoid_done, masked_done, stick_done = sem("sigmoid_done"), sem("masked_done"), sem("stick_done")
        probs_ready, probsT_psum, probsT_done = sem("probs_ready"), sem("probsT_psum"), sem("probsT_done")
        headout_done, headout_hi, headout_lo = sem("headout_done"), sem("headout_hi"), sem("headout_lo")
        rel_loaded = [sem(f"rel_loaded{p}") for p in range(2)]
        tab_loaded, tab_psum, tab_copied, tab_stored = (sem("tab_loaded"), sem("tab_psum"),
                                                        sem("tab_copied"), sem("tab_stored"))
        const_set, const_ready = sem("const_set"), sem("const_ready")
        stored = sem("stored")

        block = ctx.enter_context(nc.Block())

        def as_gu(t):
            return t[:].rearrange("p (k n) -> p k n", k=KD // 2)

        def as_qkv(t):
            return t[:].rearrange("p (k n) -> p k n", k=KD)

        def as_rows(t):
            return t[:].rearrange("p (k n) -> p k n", k=2)

        def early_wait(eng, k, early, done):
            for i, (n, a, b) in enumerate(EARLY):
                if 4 * n + a == k and b < 4:
                    eng.wait_ge(early, sum(x[2] < 4 for x in EARLY[:i + 1]))
                elif 4 * n + a == k:
                    eng.wait_ge(done, n + 1)

        def wait_block(eng, m, i):
            what, g, b = BLOCKS[i]
            if b == 0:
                eng.wait_ge(proj_done, m * 3 * GROUPS + sum(x[2] == 0 for x in BLOCKS[:i + 1]))
            else:
                eng.wait_ge(unit_used, MIX_UNIT[m] + MIX_ORDER.index((what, g)) + 1)

        def fillers(pp):
            o = [("o", g, r, half) for g in range(GROUPS) for r in range(ROWS) for half in range(2)]
            if pp < PAIRS - 2:
                at = FIRST_BLOCKS + 3 * pp
                return (BLOCKS[at:at + 3] + o)[:3], 2
            at = 4 * (pp - (PAIRS - 2)) + 1
            return o[at:at + 4], 3

        @block.sync
        def _(sp):
            def slot_free(n):
                sp.wait_ge(lo_done, n - RAW + 1)

            def load_gate_up(f, c, n, slot, wait):
                for kh in range(2):
                    s = (slot + kh) % RAW
                    if wait:
                        slot_free(n + kh)
                    dst = as_gu(raw[s])
                    for w, at in ((w_gate, 0), (w_up, CHUNK_F)):
                        src = w[f // 2, f % 2, kh * HALF:(kh + 1) * HALF, bass.ds(c * CHUNK_F, CHUNK_F)]
                        sp.dma_start(dst[:, :, at:at + CHUNK_F],
                                     src.rearrange("(k p) n -> p k n", p=P)).then_inc(raw_loaded[s], 16)

            def load_first():
                for n in range(2):
                    for load in range(2):
                        k = 2 * load
                        for w, at in ((w_gate, 0), (w_up, CHUNK_F)):
                            src = w[0, 0, (4 * n + k) * P:(4 * n + k + 2) * P, 0:CHUNK_F]
                            sp.dma_start(as_gu(raw[n])[:, k:k + 2, at:at + CHUNK_F],
                                         src.rearrange("(k p) n -> p k n", p=P)
                                         ).then_inc((early_loaded[n], raw_loaded[n])[load], 16)
                    if n == 0:
                        sp.dma_start(x[:, 1, :], x_in[0, P:SEQ, :]).then_inc(x_loaded[2], 16)

            def load_rows(w, k0, n):
                s = n % RAW
                slot_free(n)
                for kk in range(2):
                    sp.dma_start(as_rows(raw[s])[:, kk, :],
                                 w[(k0 + kk) * P:(k0 + kk + 1) * P, :]).then_inc(raw_loaded[s], 16)

            def load_ffn(f):
                n0 = FFN_UNIT[f]
                for c in range(2):
                    if n0 + 2 * c == 0:
                        load_first()
                    else:
                        load_gate_up(f, c, n0 + 2 * c, n0 + 2 * c, n0 + 2 * c >= RAW)
                with sp.Fori(1, CHUNKS // 2) as i:
                    for cc in range(2):
                        load_gate_up(f, i * 2 + cc, i * 4 + (n0 + 2 * cc), n0 + 2 * cc, wait=True)
                c = CHUNKS - 1
                load_gate_up(f, c, n0 + 2 * c, n0 + 2 * c, wait=True)
                for d in range(KF // 2):
                    load_rows(w_down[f // 2, f % 2], 2 * d, n0 + 2 * CHUNKS + d)

            def load_mixer(m):
                for u in range(UNITS_MIX):
                    n = MIX_UNIT[m] + u
                    what, g = MIX_ORDER[u]
                    if what == "o":
                        load_rows(w_o[m], 2 * g, n)
                        continue
                    s = n % RAW
                    slot_free(n)
                    at = "qkv".index(what) * D + g * GROUP * HD
                    for kh in range(2):
                        src = w_qkv[m][kh * HALF:(kh + 1) * HALF, at:at + GROUP * HD]
                        sp.dma_start(as_qkv(raw[s])[:, kh * 4:kh * 4 + 4, :],
                                     src.rearrange("(k p) n -> p k n", p=P)).then_inc(raw_loaded[s], 16)

            for m in range(DEPTH):
                load_ffn(2 * m)
                load_mixer(m)
                load_ffn(2 * m + 1)
            for r in range(ROWS):
                for half in range(2):
                    sp.wait_ge(x_ready, ((NORMS - 1) * ROWS + r) * PARTS + 2 + half)
                    rows, cols = slice(r * P, (r + 1) * P), slice(half * HALF, (half + 1) * HALF)
                    sp.dma_start(out[0, rows, cols], x[:, r, cols]).then_inc(stored, 16)
            sp.wait_ge(stored, 2 * 16 * ROWS)

        @block.tensor
        def _(pe):
            def unit_ready(n):
                pe.wait_ge(lo_done, n + 1)

            def transpose_x(t, r, pieces):
                for piece in pieces:
                    if t == 0:
                        pe.wait_ge(x_loaded[piece // 2 if r == 0 else 2], 16)
                    else:
                        pe.wait_ge(x_ready, ((t - 1) * ROWS + r) * PARTS + piece + 1)
                    if r > 0:
                        pe.wait_ge(xT_lo_done, ROWS * PARTS * t + piece + 1)
                    a, b = PIECES[piece]
                    for k in range(a, b):
                        last = pe.transpose(XT(piece)[:, (k - a) * P:(k - a + 1) * P],
                                            x[:, r, k * P:(k + 1) * P], ident[:])
                    last.then_inc(xT_psum, 1)

            def xT_ready(t, r, k):
                for piece, (a, _) in enumerate(PIECES):
                    if a == k:
                        pe.wait_ge(xT_lo_done, (ROWS * t + r) * PARTS + piece + 1)

            def three(acc, st, mv, first, last):
                pe.matmul(acc, st[0], mv[0], start=first, stop=False)
                pe.matmul(acc, st[0], mv[1], start=False, stop=False)
                return pe.matmul(acc, st[1], mv[0], start=False, stop=last)

            def static_zero(n):
                return isinstance(n, int) and n == 0

            def gate_up(r, par, slot, n, release, t=None, between=(), khs=(0, 1)):
                for kh in khs:
                    s = (slot + kh) % 4
                    if not release and not static_zero(n):
                        unit_ready(n + kh)
                    for k in range(4):
                        kk = 4 * kh + k
                        if static_zero(n) and not release:
                            early_wait(pe, kk, early_lo, lo_done)
                        for at, piece in between:
                            if at == kk:
                                transpose_x(t, 1, (piece,))
                        if t is not None:
                            xT_ready(t, r, kk)
                        rows = slice(r * P, (r + 1) * P)
                        last = three(GU[par][r], (xT_hi[:, kk, rows], xT_lo[:, kk, rows]),
                                     (as_gu(w_hi[s])[:, k, :], as_gu(w_lo[s])[:, k, :]), kk == 0, kk == KD - 1)
                    if release and kh == 0:
                        last.then_inc(unit_used, 1)
                return last

            def turn_hidden(h_wait):
                pe.wait_ge(hidden_done, h_wait)
                for j in range(2):
                    for r in range(ROWS):
                        last = pe.transpose(TURN[:, (2 * j + r) * P:(2 * j + r + 1) * P],
                                            hidden[:, r, j * P:(j + 1) * P], ident[:])
                last.then_inc(hT_psum, 1)

            def chunk_in_loop(f, i, cc):
                n0 = FFN_UNIT[f]
                n, par, slot = i * 4 + (n0 + 2 * cc), cc % 2, 2 * cc
                gate_up(0, par, slot, n, False).then_inc(gu_done, 1)
                turn_hidden(i * 4 + (f * CHUNKS * ROWS + 2 * cc))
                gate_up(1, par, slot, n, True).then_inc(unit_used, 1)

            def half_block(r, half, d, n, count, ready=None):
                s = SLOT[n]
                rows, cols = slice(r * P, (r + 1) * P), slice(half * HALF, (half + 1) * HALF)
                for kk in range(2):
                    k = 2 * d + kk
                    if ready:
                        ready(kk)
                    last = three(Y[r][half], (hT_hi[:, k, rows], hT_lo[:, k, rows]),
                                 (as_rows(w_hi[s])[:, kk, cols], as_rows(w_lo[s])[:, kk, cols]),
                                 k == 0, k == 2 * count - 1)
                return last

            def ffn_matmul(f, t, finish):
                n0 = FFN_UNIT[f]
                if f == 0:
                    gate_up(0, 0, 0, n0, False, t, FIRST_TURNS, khs=(0,))
                    gate_up(1, 0, 0, n0, True, t, khs=(0,))
                    transpose_x(t, 1, (2,))
                    gate_up(0, 0, 0, n0, False, t, khs=(1,)).then_inc(gu_done, 1)
                    relative_table()
                    gate_up(1, 0, 0, n0, True, t, khs=(1,)).then_inc(unit_used, 1)
                else:
                    gate_up(0, 0, 0, n0, False, t, LATE_TURNS if f % 2 else FFN_TURNS).then_inc(gu_done, 1)
                    transpose_x(t, 1, (2,))
                    gate_up(1, 0, 0, n0, True, t).then_inc(unit_used, 1)
                with pe.Fori(0, CHUNKS // 2) as i:
                    for cc in (1, 2):
                        chunk_in_loop(f, i, cc)
                n0, count = n0 + 2 * CHUNKS, KF // 2
                for d in range(count - HELD):
                    unit_ready(n0 + d)
                    if d == 0:
                        pe.wait_ge(hidden_done, (f * CHUNKS + CHUNKS - 1) * ROWS)
                    if d == 1:
                        turn_hidden((f + 1) * CHUNKS * ROWS)
                    pe.wait_ge(hT_lo_done, f * CHUNKS + d + 1)
                    for r in range(ROWS):
                        for half in range(2):
                            last = half_block(r, half, d, n0 + d, count)
                    last.then_inc(unit_used, 1)
                pe.wait_ge(hT_lo_done, (f + 1) * CHUNKS)
                for r in range(ROWS):
                    for half in range(2):
                        for d in range(count - HELD, count):
                            if r == 0 and half == 0:
                                unit_ready(n0 + d)
                            if r == 1 and half == 1 and d < count - 1:
                                finish([(0, 1), (2,)][d - (count - HELD)])
                            last = half_block(r, half, d, n0 + d, count)
                            if r == 1 and half == 1:
                                last.then_inc(unit_used, 1)
                        if not (r == 1 and half == 1):
                            last.then_inc(y_done, 1)

            def proj_block(m, i, t=None, between=()):
                what, g, b = BLOCKS[i]
                n = MIX_UNIT[m] + MIX_ORDER.index((what, g))
                hi, lo = as_qkv(w_hi[SLOT[n]]), as_qkv(w_lo[SLOT[n]])
                if b == 0:
                    unit_ready(n)
                if i >= 2:
                    pe.wait_ge(proj_copied, m * len(BLOCKS) + i - 1)
                acc = PROJ(i)
                part = slice(b * P, (b + 1) * P)
                for k in range(KD):
                    for at, piece in between:
                        if at == k:
                            transpose_x(t, 1, (piece,))
                    if t is not None:
                        xT_ready(t, b, k)
                    if what == "v":
                        last = three(acc, (xT_hi[:, k, part], xT_lo[:, k, part]), (hi[:, k, :], lo[:, k, :]),
                                     k == 0, k == KD - 1)
                    else:
                        last = three(acc, (hi[:, k, part], lo[:, k, part]), (xT_hi[:, k, :], xT_lo[:, k, :]),
                                     k == 0, k == KD - 1)
                last.then_inc(proj_done if b == 0 else unit_used, 1)

            def out_half(m, g, r, half):
                n = MIX_UNIT[m] + 3 * GROUPS + g
                if half == 0:
                    unit_ready(n)
                if (g, r, half) == (0, 1, 1):
                    pe.wait_ge(proj_copied, (m + 1) * len(BLOCKS))
                last = half_block(r, half, g, n, GROUPS,
                                  lambda kk: pe.wait_ge(headout_lo, m * PAIRS + 2 * g + kk + 1))
                if (r, half) == (1, 1):
                    last.then_inc(unit_used, 1)
                elif g == GROUPS - 1:
                    last.then_inc(y_done, 1)

            def scores(m, pp):
                g, p = pp // 2, pp % 2
                pe.wait_ge(proj_copied, m * len(BLOCKS) + BLOCKS.index(("k", g, p)) + 1)
                if m * PAIRS + pp > 0:
                    pe.wait_ge(probsT_done, m * PAIRS + pp)
                q, k = qT[g % 2], kT[g % 2]
                for r, (a, b) in enumerate(SPANS):
                    for h in range(2):
                        part = slice(h * HD, (h + 1) * HD)
                        last = pe.matmul(SCORES[:, h, a:b], q[part, p, r * P:(r + 1) * P], k[part, p, 0:b - a],
                                         start=True, stop=True)
                last.then_inc(scores_done, 1)

            def turn_probs(m, pp):
                pe.wait_ge(probs_ready, m * PAIRS + pp + 1)
                pr = probs[pp % 2]
                for h in range(2):
                    for to, at in ((0, 2 * P), (P, 0), (2 * P, P)):
                        last = pe.transpose(SCORES[:, h, to:to + P], pr[:, h, at:at + P], ident[:])
                last.then_inc(probsT_psum, 1)

            def head_out(m, pp):
                g, p = pp // 2, pp % 2
                pe.wait_ge(probsT_done, m * PAIRS + pp + 1)
                if m * PAIRS + pp > 0:
                    pe.wait_ge(headout_lo, m * PAIRS + pp)
                for h in range(2):
                    acc = HEADOUT[h * HD:(h + 1) * HD, :]
                    cols = slice((2 * p + h) * HD, (2 * p + h + 1) * HD)
                    pe.matmul(acc, v[g % 2][:, 0, cols], probsT[:, h, 0:2 * P], start=True, stop=False)
                    last = pe.matmul(acc[:, P:2 * P], v[g % 2][:, 1, cols], probsT[:, h, 2 * P:3 * P],
                                     start=False, stop=True)
                last.then_inc(headout_done, 1)

            def mixer_matmul(m, t, finish):
                proj_block(m, 0, t)
                proj_block(m, 1, t, MIX_TURNS)
                transpose_x(t, 1, (2,))
                proj_block(m, 2, t)
                for i in range(3, FIRST_BLOCKS):
                    proj_block(m, i)
                for pp in range(PAIRS):
                    scores(m, pp)
                    todo, turn = fillers(pp)
                    for j, block in enumerate(todo):
                        if j == turn:
                            turn_probs(m, pp)
                        if block[0] == "o":
                            out_half(m, *block[1:])
                        else:
                            proj_block(m, BLOCKS.index(block))
                    head_out(m, pp)
                last_g = GROUPS - 1
                out_half(m, last_g - 1, 0, 1)
                for half in range(2):
                    out_half(m, last_g, 0, half)
                for half in range(2):
                    out_half(m, last_g - 1, 1, half)
                out_half(m, last_g, 1, 0)
                finish((0, 1))
                out_half(m, last_g, 1, 1)
                finish((2,))

            def relative_table():
                pe.wait_ge(tab_loaded, 48)
                pe.wait_ge(const_ready, 3)
                pe.matmul(Y[1][0][0:HEADS, 0:P], tab[:, 0, :], ident[:], start=True, stop=True)
                pe.matmul(Y[1][0][0:HEADS, P:2 * P], tab[:, 1, :], ident[:], start=True, stop=True)
                pe.matmul(Y[1][0][0:HEADS, 2 * P:3 * P], tab[0:1, 2, :], ones[:], start=True,
                          stop=True).then_inc(tab_psum, 1)

            pe.wait_ge(const_ready, 2)
            for pieces, count in zip(((), (0, 1), (2,)), WARM_UP):
                transpose_x(0, 0, pieces)
                for _ in range(count):
                    pe.matmul(Y[1][1][:, 0:P], ident[:], ident[:], start=True, stop=True)
            for m in range(DEPTH):
                t = 3 * m
                ffn_matmul(2 * m, t, lambda pieces: transpose_x(t + 1, 0, pieces))
                mixer_matmul(m, t + 1, lambda pieces: transpose_x(t + 2, 0, pieces))
                ffn_matmul(2 * m + 1, t + 2,
                           lambda pieces: transpose_x(t + 3, 0, pieces) if m < DEPTH - 1 else None)

        @block.scalar
        def _(act):
            def load_table(function):
                act.activation(unread[:], power[:], function)

            def hi_part(n, raw_slot, count, slot, before):
                act.wait_ge(raw_loaded[raw_slot], count * 32)
                if before is not None:
                    act.wait_ge(unit_used, before + 1)
                act.activation(w_hi[slot][:], raw[raw_slot][:], ACT.Copy).then_inc(hi_done, 1)

            def hi_unit(n):
                if n < UNITS:
                    hi_part(n, n % RAW, n // RAW + 1, SLOT[n], former(n))

            def hi_early(parts):
                for n, a, b in parts:
                    if a % 2 == 0:
                        act.wait_ge((early_loaded[n], raw_loaded[n])[a // 2], 32)
                    act.activation(as_gu(w_hi[n])[:, a:b, :], as_gu(raw[n])[:, a:b, :],
                                   ACT.Copy).then_inc(early_hi if b < 4 else hi_done, 1)

            def silu(f, c, r, par, again=True):
                idx = c * 2 + (f * CHUNKS * ROWS + r)
                if r == 0:
                    act.wait_ge(gu_done, c + (f * CHUNKS + 1))
                else:
                    act.wait_ge(unit_used, c * 2 + (FFN_UNIT[f] + 2))
                if r == 0 and again:
                    act.wait_ge(hidden_done, idx - 1)
                act.activation(gate_act[:, r, :], GU[par][r][:, 0:CHUNK_F], ACT.Silu).then_inc(silu_done, 1)

            def hT_hi_part(f, c):
                act.wait_ge(hT_psum, c + (f * CHUNKS + 1))
                act.activation(hT_hi[:, bass.ds(c * 2, 2), :], TURN.rearrange("p (k n) -> p k n", k=2),
                               ACT.Copy).then_inc(hT_hi_done, 1)

            def xT_hi_part(t, r, pieces=range(PARTS)):
                for piece in pieces:
                    a, b = PIECES[piece]
                    act.wait_ge(xT_psum, (ROWS * t + r) * PARTS + piece + 1)
                    act.activation(xT_hi[:, a:b, r * P:(r + 1) * P],
                                   XT(piece).rearrange("p (k n) -> p k n", n=P), ACT.Copy).then_inc(xT_hi_done, 1)

            def ffn_scalar(f, t):
                n0 = FFN_UNIT[f]
                if t > 0:
                    xT_hi_part(t, 1)
                hi_unit(n0 + 2)
                silu(f, 0, 0, 0, again=False)
                if f == 0:
                    relative_table()
                hi_unit(n0 + 3)
                with act.Fori(0, CHUNKS // 2) as i:
                    for cc in (1, 2):
                        c = i * 2 + cc
                        silu(f, c - 1, 1, (cc - 1) % 2)
                        for kh in range(2):
                            j = 2 * cc + 2 + kh
                            n = n0 + j
                            hi_part(i * 4 + n, n % RAW, i + (n // RAW + 1), j % 4, i * 4 + (n - 4))
                        silu(f, c, 0, cc % 2)
                        hT_hi_part(f, c - 1)
                silu(f, CHUNKS - 1, 1, 0)
                n0 += 2 * CHUNKS
                hi_unit(n0 + 2)
                hT_hi_part(f, CHUNKS - 1)
                for d in range(3, KF // 2 + 2):
                    hi_unit(n0 + d)

            def copy_proj(m, i):
                what, g, b = BLOCKS[i]
                wait_block(act, m, i)
                if g >= 2:
                    act.wait_ge(headout_done, m * PAIRS + 2 * (g - 1))
                dst = {"v": v, "q": qT, "k": kT}[what][g % 2]
                act.activation(dst[:, b, :], PROJ(i), ACT.Copy,
                               scale=1.0 if what != "q" else -SCALE if m % 2 == 0 else SCALE
                               ).then_inc(proj_copied, 1)

            def exps(m, pp):
                par = pp % 2
                for h in range(2):
                    for r, (a, b) in enumerate(SPANS):
                        j = 2 * h + r
                        act.wait_ge(biased_done, 4 * pp + j + 1)
                        act.activation(probs[par][:, h, a:b], probs[par][:, h, a:b], ACT.Exp,
                                       bias=neg_top[:, par, j:j + 1], scale=-1.0,
                                       accum_out=total[:, par, j:j + 1]).then_inc(exp_done, 1)

            def sigmoids(m, pp):
                act.wait_ge(scores_done, m * PAIRS + pp + 1)
                if pp >= 1:
                    act.wait_ge(probs_ready, m * PAIRS + pp)
                act.activation(stick[:], SCORES, ACT.Sigmoid, scale=-1.0).then_inc(sigmoid_done, 1)
                if pp >= 2:
                    act.wait_ge(probsT_psum, m * PAIRS + pp - 1)
                act.activation(probs[pp % 2][:], SCORES, ACT.Sigmoid).then_inc(sigmoid_done, 1)

            def probsT_copy(m, pp):
                act.wait_ge(probsT_psum, m * PAIRS + pp + 1)
                if m * PAIRS + pp > 0:
                    act.wait_ge(headout_done, m * PAIRS + pp)
                act.activation(probsT[:], SCORES, ACT.Copy).then_inc(probsT_done, 1)

            def headout_hi_part(m, pp):
                act.wait_ge(headout_done, m * PAIRS + pp + 1)
                act.activation(hT_hi[:, pp, :], HEADOUT, ACT.Copy).then_inc(headout_hi, 1)

            def mixer_scalar(m, t):
                n0 = MIX_UNIT[m]
                weights = exps if m % 2 == 0 else sigmoids
                hi_unit(n0 + 2)
                copy_proj(m, 0)
                xT_hi_part(t, 1, (0, 1))
                copy_proj(m, 1)
                xT_hi_part(t, 1, (2,))
                hi_unit(n0 + 3)
                load_table(ACT.Exp if m % 2 == 0 else ACT.Sigmoid)
                copy_proj(m, 2)
                copy_proj(m, 3)
                hi_unit(n0 + 4)
                for i in range(4, FIRST_BLOCKS):
                    copy_proj(m, i)
                hi_unit(n0 + 5)
                for pp in range(PAIRS):
                    blocks = [BLOCKS.index(todo) for todo in fillers(pp)[0] if todo[0] != "o"]
                    during, after = AHEAD[pp]
                    weights(m, pp)
                    for j, i in enumerate(blocks[0:2]):
                        copy_proj(m, i)
                        if j == 0 and during:
                            hi_unit(n0 + during)
                    probsT_copy(m, pp)
                    if after:
                        hi_unit(n0 + after)
                    for i in blocks[2:]:
                        copy_proj(m, i)
                    headout_hi_part(m, pp)
                load_table(ACT.Silu)

            def relative_table():
                act.wait_ge(tab_psum, 1)
                act.activation(tab_row[:], Y[1][0][0:HEADS, 0:3 * P], ACT.Copy, scale=-1.0).then_inc(tab_copied, 1)

            for half in range(2):
                cols = slice(half * HALF, (half + 1) * HALF)
                act.dma_start(x[:, 0, cols], x_in[0, 0:P, cols]).then_inc(x_loaded[half], 16)
            act.wait_ge(const_ready, 1)
            load_table(ACT.Silu)
            xT_hi_part(0, 0, (0,))
            hi_early(EARLY[0:1])
            xT_hi_part(0, 0, (1,))
            hi_early(EARLY[1:2])
            xT_hi_part(0, 0, (2,))
            hi_early(EARLY[2:4])
            xT_hi_part(0, 1, (0, 1))
            hi_early(EARLY[4:])
            xT_hi_part(0, 1, (2,))
            for m in range(DEPTH):
                ffn_scalar(2 * m, 3 * m)
                xT_hi_part(3 * m + 1, 0)
                mixer_scalar(m, 3 * m + 1)
                xT_hi_part(3 * m + 2, 0)
                ffn_scalar(2 * m + 1, 3 * m + 2)
                if m < DEPTH - 1:
                    xT_hi_part(3 * m + 3, 0)

        @block.vector
        def _(dve):
            def lo_part(n, raw_slot, slot):
                dve.wait_ge(hi_done, n + 1)
                dve.tensor_tensor(w_lo[slot][:], raw[raw_slot][:], w_hi[slot][:], ALU.subtract).then_inc(lo_done, 1)

            def lo_unit(n):
                if n < UNITS:
                    lo_part(n, n % RAW, SLOT[n])

            def lo_early(parts):
                for n, a, b in parts:
                    early_wait(dve, 4 * n + a, early_hi, hi_done)
                    dve.tensor_tensor(as_gu(w_lo[n])[:, a:b, :], as_gu(raw[n])[:, a:b, :], as_gu(w_hi[n])[:, a:b, :],
                                      ALU.subtract).then_inc(early_lo if b < 4 else lo_done, 1)

            def hidden_rows(f, c, r, par, first=False):
                idx = c * 2 + (f * CHUNKS * ROWS + r)
                dve.wait_ge(silu_done, idx + 1)
                if not first:
                    dve.wait_ge(hT_psum, c + f * CHUNKS)
                dve.tensor_tensor(hidden[:, r, :], GU[par][r][:, CHUNK_F:], gate_act[:, r, :],
                                  ALU.mult).then_inc(hidden_done, 1)

            def hT_lo_part(f, c):
                dve.wait_ge(hT_hi_done, c + (f * CHUNKS + 1))
                dve.tensor_tensor(hT_lo[:, bass.ds(c * 2, 2), :], TURN.rearrange("p (k n) -> p k n", k=2),
                                  hT_hi[:, bass.ds(c * 2, 2), :], ALU.subtract).then_inc(hT_lo_done, 1)

            def xT_lo_part(t, r, pieces=range(PARTS)):
                for piece in pieces:
                    a, b = PIECES[piece]
                    dve.wait_ge(xT_hi_done, (ROWS * t + r) * PARTS + piece + 1)
                    dst = (slice(None), slice(a, b), slice(r * P, (r + 1) * P))
                    dve.tensor_tensor(xT_lo[dst], XT(piece).rearrange("p (k n) -> p k n", n=P), xT_hi[dst],
                                      ALU.subtract).then_inc(xT_lo_done, 1)

            def norm(l, r, split_too=False):
                scale, eps = NORM_SCALE[l]
                at = ROWS * l + r
                halves = [slice(half * HALF, (half + 1) * HALF) for half in range(2)]
                for half, cols in enumerate(halves):
                    if r == 1 and half == 1:
                        dve.wait_ge(unit_used, NORM_UNIT[l])
                    else:
                        dve.wait_ge(y_done, 3 * l + 2 * r + half + 1)
                    dve.scalar_tensor_tensor(x[:, r, cols], x[:, r, cols], scale, Y[r][half],
                                             ALU.mult, ALU.add).then_inc(resid_done, 1)
                    dve.wait_ge(resid_done, 2 * at + half + 1)
                    dve.bn_stats(stats[:, half, :], x[:, r, cols]).then_inc(stats_done, 1)
                    if half == 0 and split_too:
                        xT_lo_part(l + 1, 0, (2,))
                dve.wait_ge(stats_done, 2 * at + 2)
                dve.bn_aggr(mean_var[:], stats[:].rearrange("p a b -> p (a b)")).then_inc(mean_done, 1)
                dve.wait_ge(mean_done, at + 1)
                dve.tensor_scalar(var_eps[:], mean_var[:, 1:2], eps, None, ALU.add).then_inc(eps_done, 1)
                dve.wait_ge(norm_loaded, 32 * (l + 1))
                pieces = [slice(a * P, b * P) for a, b in PIECES]

                def gained(piece):
                    cols = pieces[piece]
                    dve.scalar_tensor_tensor(x[:, r, cols], x[:, r, cols], mean_var[:, 0:1], gain[:, cols],
                                             ALU.subtract, ALU.mult).then_inc(gained_done, 1)

                def finished(piece):
                    cols = pieces[piece]
                    if piece == 0:
                        dve.wait_ge(rstd_done, at + 1)
                    dve.wait_ge(gained_done, PARTS * at + piece + 1)
                    dve.scalar_tensor_tensor(x[:, r, cols], x[:, r, cols], rstd[:, 0:1], shift[:, cols],
                                             ALU.mult, ALU.add).then_inc(x_ready, 1)

                gained(0)
                gained(1)
                finished(0)
                finished(1)
                gained(2)
                if split_too:
                    xT_lo_part(l + 1, r, (0,))
                finished(2)
                if split_too:
                    xT_lo_part(l + 1, r, (1, 2))

            def ffn_vector(f, t):
                n0 = FFN_UNIT[f]
                if t > 0:
                    norm(t - 1, 1, split_too=True)
                lo_unit(n0 + 2)
                hidden_rows(f, 0, 0, 0, first=True)
                lo_unit(n0 + 3)
                with dve.Fori(0, CHUNKS // 2) as i:
                    for cc in (1, 2):
                        c = i * 2 + cc
                        hidden_rows(f, c - 1, 1, (cc - 1) % 2, first=True)
                        j = 2 * cc + 2
                        lo_part(i * 4 + (n0 + j), (n0 + j) % RAW, j % 4)
                        hidden_rows(f, c, 0, cc % 2)
                        lo_part(i * 4 + (n0 + j + 1), (n0 + j + 1) % RAW, (j + 1) % 4)
                        hT_lo_part(f, c - 1)
                hidden_rows(f, CHUNKS - 1, 1, 0)
                n0 += 2 * CHUNKS
                lo_unit(n0 + 2)
                hT_lo_part(f, CHUNKS - 1)
                for d in range(3, KF // 2 + 2):
                    lo_unit(n0 + d)
                norm(FFN_NORM[f], 0)

            def soften(m, pp):
                par = pp % 2
                dve.wait_ge(scores_done, m * PAIRS + pp + 1)
                dve.wait_ge(rel_loaded[par], 32 * (pp // 2 + 1))
                if pp >= 2:
                    dve.wait_ge(probsT_psum, pp - 1)
                    dve.wait_ge(exp_done, 4 * (pp - 1))
                for h in range(2):
                    for r, (a, b) in enumerate(SPANS):
                        j = 2 * h + r
                        dve.tensor_tensor_reduce(probs[par][:, h, a:b], SCORES[:, h, a:b],
                                                 rel[par][:, h, 0:b - a][:, ::-1], 1.0, 3.0e38, ALU.add, ALU.min,
                                                 neg_top[:, par, j:j + 1]).then_inc(biased_done, 1)

            def normalise(m, pp):
                par = pp % 2
                dve.wait_ge(exp_done, 4 * (pp + 1))
                dve.reciprocal(inv_total[:, par, :], total[:, par, :]).then_inc(inv_done, 1)
                dve.wait_ge(inv_done, pp + 1)
                for h in range(2):
                    for r, (a, b) in enumerate(SPANS):
                        j = 2 * h + r
                        last = dve.tensor_scalar(probs[par][:, h, a:b], probs[par][:, h, a:b],
                                                 inv_total[:, par, j:j + 1], None, ALU.mult)
                last.then_inc(probs_ready, 1)

            def sticks(m, pp):
                dve.wait_ge(masked_done, 2 * pp + 1)
                for h in range(2):
                    dve.tensor_tensor_scan(stick[:, h, ::-1], stick[:, h, ::-1], restart[:, ::-1], 1.0,
                                           ALU.mult, ALU.max).then_inc(stick_done, 1)

            def break_sticks(m, pp):
                dve.wait_ge(masked_done, 2 * pp + 2)
                dve.wait_ge(stick_done, 2 * pp + 2)
                dve.tensor_tensor(probs[pp % 2][:, :, 0:KEYS - 1], probs[pp % 2][:, :, 0:KEYS - 1],
                                  stick[:, :, 1:KEYS], ALU.mult).then_inc(probs_ready, 1)

            def headout_lo_part(m, pp):
                dve.wait_ge(headout_hi, m * PAIRS + pp + 1)
                dve.tensor_tensor(hT_lo[:, pp, :], HEADOUT, hT_hi[:, pp, :],
                                  ALU.subtract).then_inc(headout_lo, 1)

            def mixer_vector(m, t):
                n0 = MIX_UNIT[m]
                norm(t - 1, 1, split_too=True)
                for n in range(n0 + 2, n0 + 5):
                    lo_unit(n)
                before = 5
                for pp in range(PAIRS):
                    if m % 2 == 0:
                        soften(m, pp)
                    if before and pp < PAIRS - 2:
                        lo_unit(n0 + before)
                    if m % 2 == 0:
                        normalise(m, pp)
                    else:
                        sticks(m, pp)
                        break_sticks(m, pp)
                    during = AHEAD[pp][0] if pp < PAIRS - 2 else before
                    if during:
                        lo_unit(n0 + during)
                    headout_lo_part(m, pp)
                    before = AHEAD[pp][1]
                norm(t, 0)

            xT_lo_part(0, 0, (0,))
            lo_early(EARLY[0:1])
            xT_lo_part(0, 0, (1,))
            lo_early(EARLY[1:2])
            xT_lo_part(0, 0, (2,))
            lo_early(EARLY[2:4])
            xT_lo_part(0, 1, (0, 1))
            lo_early(EARLY[4:])
            xT_lo_part(0, 1, (2,))
            for m in range(DEPTH):
                ffn_vector(2 * m, 3 * m)
                xT_lo_part(3 * m + 1, 0, (0, 1))
                mixer_vector(m, 3 * m + 1)
                xT_lo_part(3 * m + 2, 0, (0, 1))
                ffn_vector(2 * m + 1, 3 * m + 2)
                if m < DEPTH - 1:
                    xT_lo_part(3 * m + 3, 0, (0, 1))
            norm(NORMS - 1, 1)

        @block.gpsimd
        def _(pool):
            def load_norm(l):
                for dst, src in ((gain, ln_g), (shift, ln_b)):
                    row = src[l // 3, l % 3:l % 3 + 1, :]
                    pool.dma_start(dst[:], row.to_broadcast([P, D])).then_inc(norm_loaded, 16)

            def norm(l, r):
                at = ROWS * l + r
                pool.wait_ge(eps_done, at + 1)
                pool.tensor_tensor(rstd[:], var_eps[:], power[:], ALU.pow).then_inc(rstd_done, 1)

            def load_rel(pp):
                for row, col in ((0, ATT_CHUNK), (ATT_CHUNK, 0)):
                    src = bass.AP(tensor=table.tensor, offset=2 * pp * 3 * P + 1 + row + col,
                                  ap=[[1, ATT_CHUNK], [3 * P, 2], [1, 2 * P - col]])
                    pool.dma_start(rel[pp % 2][row:row + ATT_CHUNK, :, col:], src).then_inc(rel_loaded[pp % 2], 16)

            pool.memset(power[:], -0.5).then_inc(const_ready, 1)
            pool.memset(ident[:], 0.0).then_inc(const_set, 1)
            pool.wait_ge(const_set, 1)
            pool.affine_select(ident[:], ident[:], pattern=[[-1, P]], compare_op=ALU.not_equal, fill=1.0,
                               base=0, channel_multiplier=1).then_inc(const_ready, 1)
            pool.memset(ones[:], 1.0).then_inc(const_ready, 1)
            pool.memset(restart[:], 0.0).then_inc(const_set, 1)
            pool.wait_ge(const_set, 2)
            for a, b in SPANS:
                pool.memset(restart[:, b - 1:b], 1.0).then_inc(const_set, 1)
            for p in range(2):
                pool.memset(rel[p][0:ATT_CHUNK, :, 0:ATT_CHUNK], MASKED).then_inc(const_set, 1)
            pool.dma_start(tab[:, 0:2, :], rel_bias[0:2 * P, :].rearrange("(t p) h -> p t h", p=P)).then_inc(tab_loaded, 32)
            pool.dma_start(tab[0:1, 2, :], rel_bias[2 * P:2 * P + 1, :]).then_inc(tab_loaded, 16)
            pool.wait_ge(tab_copied, 1)
            pool.dma_start(table, tab_row[:]).then_inc(tab_stored, 16)
            pool.wait_ge(tab_stored, 16)
            pool.wait_ge(const_set, 6)
            load_rel(0)
            load_rel(1)
            load_norm(0)
            for l in range(NORMS):
                for r in range(ROWS):
                    norm(l, r)
                if l + 1 < NORMS:
                    pool.wait_ge(x_ready, PARTS * ROWS * (l + 1))
                    load_norm(l + 1)
                if l == 0:
                    for pp in range(2, PAIRS):
                        pool.wait_ge(biased_done, 4 * (pp - 1))
                        load_rel(pp)
                if l == 3:
                    for pp in range(PAIRS):
                        for k, (t, fill) in enumerate(((stick, 1.0), (probs[pp % 2], 0.0))):
                            pool.wait_ge(sigmoid_done, 2 * pp + k + 1)
                            d = t[:, :, DIAG:].rearrange("p h (b n) -> p h b n", b=2)
                            pool.affine_select(d, d, pattern=[[0, 2], [0, 2], [-1, P]], compare_op=ALU.is_gt,
                                               fill=fill, base=0, channel_multiplier=1).then_inc(masked_done, 1)


def kernel(x, w_qkv_a, w_o_a, rel_bias, w_qkv_b, w_o_b, ffn_w_gate, ffn_w_up, ffn_w_down, ln_g, ln_b):
    import numpy as np
    import concourse.bacc as bacc
    from concourse.bass_utils import run_bass_kernel_spmd

    nc = bacc.Bacc("TRN2", target_bir_lowering=False, num_devices=1)
    given = dict(x=x, w_qkv_a=w_qkv_a, w_o_a=w_o_a, rel_bias=rel_bias, w_qkv_b=w_qkv_b, w_o_b=w_o_b,
                 ffn_w_gate=ffn_w_gate, ffn_w_up=ffn_w_up, ffn_w_down=ffn_w_down, ln_g=ln_g, ln_b=ln_b)
    arrays = {"in_" + name: np.ascontiguousarray(a) for name, a in given.items()}
    t = {name[3:]: nc.dram_tensor(name, a.shape, F32, kind="ExternalInput").ap() for name, a in arrays.items()}
    table = nc.dram_tensor("bias_by_distance", (HEADS, 3 * P), F32, kind="Internal").ap()
    out = nc.dram_tensor("out", (1, SEQ, D), F32, kind="ExternalOutput").ap()
    build(nc, t["x"], (t["w_qkv_a"][0], t["w_qkv_b"][0]), (t["w_o_a"][0], t["w_o_b"][0]), t["rel_bias"],
          t["ffn_w_gate"], t["ffn_w_up"], t["ffn_w_down"], t["ln_g"], t["ln_b"], table, out)
    return run_bass_kernel_spmd(nc, [arrays], core_ids=[0]).results[0]["out"]
```
